# Optimizing a Trainium2 kernel written in Bass

```python
import math
import jax, jax.numpy as jnp
from jax import lax
import numpy as np

D_MODEL = 1024
BATCH = 1
SEQ = 256
DEPTH = 1

CHUNK = 64
LEFT_CHUNKS = 8
BAND = LEFT_CHUNKS + 1
N_HEADS = 16
HEAD_DIM = 64
D_ATTN = N_HEADS * HEAD_DIM
MAX_REL = 128
D_RNN = D_MODEL
N_RG_BLOCKS = 16
RG_BLOCK = D_RNN // N_RG_BLOCKS
CONV_W = 4
RG_C = 8.0
D_FF = ((8 * D_MODEL // 3 + 255) // 256) * 256
IN_COLS = 3 * D_ATTN + 2 * D_RNN + 2 * D_MODEL
EPS = 1e-6
NEG_INF = -1e30


def rmsnorm(x, g):
    xf = x.astype(jnp.float32)
    var = jnp.mean(xf * xf, axis=-1, keepdims=True)
    return (xf * lax.rsqrt(var + EPS) * g.astype(jnp.float32)).astype(x.dtype)

def rel_bias_band(table):
    i = jnp.arange(CHUNK)[:, None]
    m = jnp.arange(BAND * CHUNK)[None, :]
    dist = i - m + LEFT_CHUNKS * CHUNK
    idx = jnp.clip(dist, -MAX_REL, MAX_REL) + MAX_REL
    return table[:, idx]

def chunked_band_attention(q, k, v, rel_table):
    B, S, _ = q.shape
    nc = S // CHUNK
    q = q.reshape(B, nc, CHUNK, N_HEADS, HEAD_DIM)
    k = k.reshape(B, nc, CHUNK, N_HEADS, HEAD_DIM)
    v = v.reshape(B, nc, CHUNK, N_HEADS, HEAD_DIM)
    pad = jnp.zeros((B, LEFT_CHUNKS, CHUNK, N_HEADS, HEAD_DIM), k.dtype)
    kp = jnp.concatenate([pad, k], axis=1)
    vp = jnp.concatenate([pad, v], axis=1)
    kb = jnp.concatenate([kp[:, j:j + nc] for j in range(BAND)], axis=2)
    vb = jnp.concatenate([vp[:, j:j + nc] for j in range(BAND)], axis=2)
    scale = 1.0 / math.sqrt(HEAD_DIM)
    s = jnp.einsum('bnqhd,bnkhd->bhnqk', q, kb).astype(jnp.float32) * scale
    s = s + rel_bias_band(rel_table).astype(jnp.float32)[None, :, None, :, :]
    key_chunk = jnp.arange(nc)[:, None] - LEFT_CHUNKS + (jnp.arange(BAND * CHUNK)[None, :] // CHUNK)
    valid = key_chunk >= 0
    s = jnp.where(valid[None, None, :, None, :], s, NEG_INF)
    p = jax.nn.softmax(s, axis=-1).astype(v.dtype)
    o = jnp.einsum('bhnqk,bnkhd->bnqhd', p, vb)
    return o.reshape(B, S, D_ATTN)

def causal_depthwise_conv(x, w, b):
    S = x.shape[1]
    xp = jnp.pad(x, ((0, 0), (CONV_W - 1, 0), (0, 0)))
    y = sum(xp[:, j:j + S] * w[j] for j in range(CONV_W))
    return y + b

def rg_lru(x, w_r, b_r, w_i, b_i, lam):
    B, S, D = x.shape
    xb = x.reshape(B, S, N_RG_BLOCKS, RG_BLOCK)
    r = jax.nn.sigmoid(jnp.einsum('bsnd,nde->bsne', xb, w_r).reshape(B, S, D) + b_r)
    i = jax.nn.sigmoid(jnp.einsum('bsnd,nde->bsne', xb, w_i).reshape(B, S, D) + b_i)
    log_a = -RG_C * r.astype(jnp.float32) * jax.nn.softplus(-lam.astype(jnp.float32))
    a = jnp.exp(log_a)
    mult = jnp.sqrt(-jnp.expm1(2.0 * log_a))
    bx = mult * (i * x).astype(jnp.float32)

    def combine(left, right):
        a1, b1 = left
        a2, b2 = right
        return a1 * a2, a2 * b1 + b2

    _, h = lax.associative_scan(combine, (a, bx), axis=1)
    return h.astype(x.dtype)

def first_inputs(seed: int = 0) -> dict:
    key = jax.random.key(seed)
    ks = jax.random.split(key, 20)
    L = DEPTH

    def nrm(k, shape, fan_in):
        return jax.random.normal(k, shape, jnp.float32) * (fan_in ** -0.5)

    x = jax.random.normal(ks[0], (BATCH, SEQ, D_MODEL), jnp.float32)
    norm_mix_g = 1.0 + 0.05 * jax.random.normal(ks[1], (L, D_MODEL), jnp.float32)
    w_in = nrm(ks[2], (L, D_MODEL, IN_COLS), D_MODEL)
    b_merge = 0.01 * jax.random.normal(ks[3], (L, 2 * D_MODEL), jnp.float32)
    rel_table = 0.5 * jax.random.normal(ks[4], (L, N_HEADS, 2 * MAX_REL + 1), jnp.float32)
    w_attn_out = nrm(ks[5], (L, D_ATTN, D_MODEL), D_ATTN)
    conv_w = nrm(ks[6], (L, CONV_W, D_RNN), CONV_W)
    conv_b = 0.01 * jax.random.normal(ks[7], (L, D_RNN), jnp.float32)
    w_rg_r = nrm(ks[8], (L, N_RG_BLOCKS, RG_BLOCK, RG_BLOCK), RG_BLOCK)
    b_rg_r = 0.01 * jax.random.normal(ks[9], (L, D_RNN), jnp.float32)
    w_rg_i = nrm(ks[10], (L, N_RG_BLOCKS, RG_BLOCK, RG_BLOCK), RG_BLOCK)
    b_rg_i = 0.01 * jax.random.normal(ks[11], (L, D_RNN), jnp.float32)
    u = jax.random.uniform(ks[12], (L, D_RNN), jnp.float32, 0.9, 0.999)
    a0 = u ** (1.0 / RG_C)
    rg_lambda = jnp.log(a0) - jnp.log1p(-a0)
    w_rnn_out = nrm(ks[13], (L, D_RNN, D_MODEL), D_RNN)
    w_o = nrm(ks[14], (L, D_MODEL, D_MODEL), D_MODEL)
    norm_ffn_g = 1.0 + 0.05 * jax.random.normal(ks[15], (L, D_MODEL), jnp.float32)
    w_ffn_in = nrm(ks[16], (L, D_MODEL, 2 * D_FF), D_MODEL)
    w_ffn_out = nrm(ks[17], (L, D_FF, D_MODEL), D_FF)
    final_norm_g = 1.0 + 0.05 * jax.random.normal(ks[18], (D_MODEL,), jnp.float32)
    return {"x": x, "norm_mix_g": norm_mix_g, "w_in": w_in, "b_merge": b_merge,
            "rel_table": rel_table, "w_attn_out": w_attn_out, "conv_w": conv_w,
            "conv_b": conv_b, "w_rg_r": w_rg_r, "b_rg_r": b_rg_r, "w_rg_i": w_rg_i,
            "b_rg_i": b_rg_i, "rg_lambda": rg_lambda, "w_rnn_out": w_rnn_out, "w_o": w_o,
            "norm_ffn_g": norm_ffn_g, "w_ffn_in": w_ffn_in, "w_ffn_out": w_ffn_out,
            "final_norm_g": final_norm_g}

def first_block(x, norm_mix_g, w_in, b_merge, rel_table, w_attn_out, conv_w, conv_b,
              w_rg_r, b_rg_r, w_rg_i, b_rg_i, rg_lambda, w_rnn_out, w_o,
              norm_ffn_g, w_ffn_in, w_ffn_out, final_norm_g):
    h = x
    splits = [D_ATTN, 2 * D_ATTN, 3 * D_ATTN, 3 * D_ATTN + D_RNN,
              3 * D_ATTN + 2 * D_RNN, 3 * D_ATTN + 2 * D_RNN + D_MODEL]
    for l in range(DEPTH):
        xn = rmsnorm(h, norm_mix_g[l])
        u = jnp.einsum('bsd,de->bse', xn, w_in[l])
        q, k, v, xr, gr, ga, gb = jnp.split(u, splits, axis=-1)
        ya = chunked_band_attention(q, k, v, rel_table[l]) @ w_attn_out[l]
        xc = causal_depthwise_conv(xr, conv_w[l], conv_b[l])
        hr = rg_lru(xc, w_rg_r[l], b_rg_r[l], w_rg_i[l], b_rg_i[l], rg_lambda[l])
        yb = (hr * jax.nn.gelu(gr)) @ w_rnn_out[l]
        gates = jax.nn.sigmoid(jnp.concatenate([ga, gb], axis=-1) + b_merge[l])
        g_a, g_b = jnp.split(gates, 2, axis=-1)
        h = h + (g_a * ya + g_b * yb) @ w_o[l]
        hn = rmsnorm(h, norm_ffn_g[l])
        gu = hn @ w_ffn_in[l]
        g, up = jnp.split(gu, 2, axis=-1)
        h = h + (jax.nn.silu(g) * up) @ w_ffn_out[l]
    return rmsnorm(h, final_norm_g)


DEPTH_2 = 2

N_A = DEPTH_2 // 2
N_B = DEPTH_2 - N_A

D_FF_2 = ((8 * D_MODEL // 3 + 127) // 128) * 128
FFN_RES_SCALE = 0.5

D_A = 2 * D_MODEL
CHUNK_2 = 128
SGU_GROUPS = 8
SGU_GROUP_DIM = D_A // SGU_GROUPS

SB_HEADS = 16
SB_HEAD_DIM = D_MODEL // SB_HEADS
SB_KV_HEADS = 4
SB_GROUP = SB_HEADS // SB_KV_HEADS
Q_BLOCK = 128

NORM_EPS = 1e-6
LN_EPS = 1e-5


def rms_norm(x, g):
    xf = x.astype(jnp.float32)
    y = xf * lax.rsqrt(jnp.mean(xf * xf, axis=-1, keepdims=True) + NORM_EPS)
    return (y * g.astype(jnp.float32)).astype(x.dtype)

def layer_norm(x, g, b):
    xf = x.astype(jnp.float32)
    mu = jnp.mean(xf, axis=-1, keepdims=True)
    xc = xf - mu
    var = jnp.mean(xc * xc, axis=-1, keepdims=True)
    y = xc * lax.rsqrt(var + LN_EPS) * g.astype(jnp.float32) + b.astype(jnp.float32)
    return y.astype(x.dtype)

def swiglu(h, w_in, w_out):
    gu = h @ w_in
    gate, up = jnp.split(gu, 2, axis=-1)
    return (jax.nn.silu(gate) * up) @ w_out

def chunked_sgu(h, w_in, ln_g, ln_b, w_s, b_s, w_out):
    B, S, _ = h.shape
    z = jax.nn.gelu(h @ w_in)
    u, v = jnp.split(z, 2, axis=-1)
    v = layer_norm(v, ln_g, ln_b)
    v = v.reshape(B, S // CHUNK_2, CHUNK_2, SGU_GROUPS, SGU_GROUP_DIM)
    causal = jnp.tril(jnp.ones((CHUNK_2, CHUNK_2), dtype=w_s.dtype))
    ws = w_s * causal[None]
    v = jnp.einsum('gts,bnsgc->bntgc', ws, v) + b_s.T[None, None, :, :, None]
    v = v.reshape(B, S, D_A)
    return (u * v) @ w_out

def stick_breaking_attention(q, k, v):
    B, S = q.shape[0], q.shape[1]
    nb = S // Q_BLOCK
    scale = 1.0 / math.sqrt(SB_HEAD_DIM)
    qf = (q.astype(jnp.float32) * scale).reshape(B, nb, Q_BLOCK, SB_KV_HEADS, SB_GROUP, SB_HEAD_DIM)
    qf = jnp.moveaxis(qf, 1, 0)
    kf = k.astype(jnp.float32)
    vf = v.astype(jnp.float32)
    key_pos = jnp.arange(S)

    def one_block(args):
        qb, bi = args
        q_pos = bi * Q_BLOCK + jnp.arange(Q_BLOCK)
        mask = key_pos[None, :] < q_pos[:, None]
        z = jnp.einsum('bqkgd,bskd->bkgqs', qb, kf)
        log_1m_beta = jnp.where(mask, jax.nn.log_sigmoid(-z), 0.0)
        rev = lax.cumsum(log_1m_beta, axis=4, reverse=True)
        excl = jnp.concatenate([rev[..., 1:], jnp.zeros_like(rev[..., :1])], axis=-1)
        a = jnp.where(mask, jnp.exp(jax.nn.log_sigmoid(z) + excl), 0.0)
        o = jnp.einsum('bkgqs,bskd->bqkgd', a, vf)
        return o.reshape(B, Q_BLOCK, SB_HEADS * SB_HEAD_DIM)

    o = lax.map(one_block, (qf, jnp.arange(nb)))
    o = jnp.moveaxis(o, 0, 1).reshape(B, S, SB_HEADS * SB_HEAD_DIM)
    return o.astype(q.dtype)

def second_inputs(seed: int = 0) -> dict:
    key = jax.random.key(seed)
    ks = jax.random.split(key, 20)
    f32 = jnp.float32
    nrm = lambda k, shape, fan_in: jax.random.normal(k, shape, f32) * (fan_in ** -0.5)
    gain = lambda k, shape: 1.0 + 0.02 * jax.random.normal(k, shape, f32)
    HD = SB_HEADS * SB_HEAD_DIM
    KVD = SB_KV_HEADS * SB_HEAD_DIM
    return {
        "x": jax.random.normal(ks[0], (BATCH, SEQ, D_MODEL), f32),
        "ffn_norm": gain(ks[1], (DEPTH_2, 2, D_MODEL)),
        "ffn_w_in": nrm(ks[2], (DEPTH_2, 2, D_MODEL, 2 * D_FF_2), D_MODEL),
        "ffn_w_out": nrm(ks[3], (DEPTH_2, 2, D_FF_2, D_MODEL), D_FF_2),
        "mix_norm": gain(ks[4], (DEPTH_2, D_MODEL)),
        "a_w_in": nrm(ks[5], (N_A, D_MODEL, 2 * D_A), D_MODEL),
        "a_ln_g": gain(ks[6], (N_A, D_A)),
        "a_ln_b": 0.02 * jax.random.normal(ks[7], (N_A, D_A), f32),
        "a_w_s": 0.5 * nrm(ks[8], (N_A, SGU_GROUPS, CHUNK_2, CHUNK_2), CHUNK_2),
        "a_b_s": gain(ks[9], (N_A, SGU_GROUPS, CHUNK_2)),
        "a_w_out": nrm(ks[10], (N_A, D_A, D_MODEL), D_A),
        "kv_norm": gain(ks[11], (D_MODEL,)),
        "w_kv": nrm(ks[12], (D_MODEL, 2 * KVD), D_MODEL),
        "b_w_q": nrm(ks[13], (N_B, D_MODEL, HD), D_MODEL),
        "b_w_o": nrm(ks[14], (N_B, HD, D_MODEL), HD),
        "final_norm": gain(ks[15], (D_MODEL,)),
    }

def second_block(x, ffn_norm, ffn_w_in, ffn_w_out, mix_norm, a_w_in, a_ln_g, a_ln_b, a_w_s,
              a_b_s, a_w_out, kv_norm, w_kv, b_w_q, b_w_o, final_norm):
    B, S, _ = x.shape
    k_shared = None
    v_shared = None
    for i in range(DEPTH_2):
        if i == N_A:
            kv = rms_norm(x, kv_norm) @ w_kv
            k_flat, v_flat = jnp.split(kv, 2, axis=-1)
            k_shared = k_flat.reshape(B, S, SB_KV_HEADS, SB_HEAD_DIM)
            v_shared = v_flat.reshape(B, S, SB_KV_HEADS, SB_HEAD_DIM)
        x = x + FFN_RES_SCALE * swiglu(rms_norm(x, ffn_norm[i, 0]), ffn_w_in[i, 0], ffn_w_out[i, 0])
        h = rms_norm(x, mix_norm[i])
        if i < N_A:
            x = x + chunked_sgu(h, a_w_in[i], a_ln_g[i], a_ln_b[i], a_w_s[i], a_b_s[i], a_w_out[i])
        else:
            j = i - N_A
            q = (h @ b_w_q[j]).reshape(B, S, SB_HEADS, SB_HEAD_DIM)
            x = x + stick_breaking_attention(q, k_shared, v_shared) @ b_w_o[j]
        x = x + FFN_RES_SCALE * swiglu(rms_norm(x, ffn_norm[i, 1]), ffn_w_in[i, 1], ffn_w_out[i, 1])
    return rms_norm(x, final_norm)


def setup_inputs(seed=0):
    out = dict(first_inputs(seed))
    for name, value in second_inputs(seed + 1).items():
        if name != "x":
            out[name + "_2"] = value
    return out


def reference(
    x, norm_mix_g, w_in, b_merge, rel_table, w_attn_out, conv_w, conv_b, w_rg_r, b_rg_r, w_rg_i,
    b_rg_i, rg_lambda, w_rnn_out, w_o, norm_ffn_g, w_ffn_in, w_ffn_out, final_norm_g,
    ffn_norm_2, ffn_w_in_2, ffn_w_out_2, mix_norm_2, a_w_in_2, a_ln_g_2, a_ln_b_2, a_w_s_2,
    a_b_s_2, a_w_out_2, kv_norm_2, w_kv_2, b_w_q_2, b_w_o_2, final_norm_2,
):
    x = first_block(
        x, norm_mix_g, w_in, b_merge, rel_table, w_attn_out, conv_w, conv_b, w_rg_r, b_rg_r,
        w_rg_i, b_rg_i, rg_lambda, w_rnn_out, w_o, norm_ffn_g, w_ffn_in, w_ffn_out,
        final_norm_g,
    )
    return second_block(
        x, ffn_norm_2, ffn_w_in_2, ffn_w_out_2, mix_norm_2, a_w_in_2, a_ln_g_2, a_ln_b_2,
        a_w_s_2, a_b_s_2, a_w_out_2, kv_norm_2, w_kv_2, b_w_q_2, b_w_o_2, final_norm_2,
    )


_drawn_inputs = setup_inputs


def setup_inputs(seed=0):
    import zlib

    import numpy as np

    out = dict(_drawn_inputs(seed))
    spreads = {}
    factors = {'b_merge': 25.842,
     'conv_b': 3.2,
     'b_rg_r': 45.292,
     'b_rg_i': 30.01,
     'ffn_norm_2': 3.855,
     'mix_norm_2': 3.931,
     'a_ln_g_2': 32.289,
     'a_ln_b_2': 32.185,
     'a_b_s_2': 4.838,
     'kv_norm_2': 19.639,
     'final_norm_2': 8.295}
    for name, (base, spread) in spreads.items():
        noise = np.random.default_rng([zlib.crc32(name.encode()), seed]).standard_normal(out[name].shape)
        drawn = base * np.exp(spread * noise) if base else spread * noise
        out[name] = __import__('jax').numpy.asarray(drawn.astype(out[name].dtype))
    for name, factor in factors.items():
        out[name] = (out[name] * factor).astype(out[name].dtype)
    return out
```

```python
from contextlib import ExitStack

import concourse.bass as bass
from concourse import mybir

F32 = mybir.dt.float32
F32R = mybir.dt.float32r
ALU = mybir.AluOpType
ACT = mybir.ActivationFunctionType
AX = mybir.AxisListType.X

P = 128
D = 1024
S = 256
NH = S // P
KD = D // P
DFF = 2816
GW = 256
NJ = DFF // GW
HEADS = 16
HD = 64
EPS = 1e-6
LN_EPS = 1e-5
NEG = -1e30
TAB = 384
DA = 2 * D
NG = 8
NKV = 4
GRP = HEADS // NKV

RING = 3
CH = 2048

C_IN = 0
C_AO = C_IN + 28
C_RO = C_AO + 4
C_WO = C_RO + 4
C_F0 = C_WO + 4
C_F1 = C_F0 + 3 * NJ
C_AI = C_F1 + 3 * NJ
C_AW = C_AI + 16
C_F2 = C_AW + 8
C_KV = C_F2 + 3 * NJ
C_F3 = C_KV + 2
C_Q = C_F3 + 3 * NJ
C_BO = C_Q + 4
C_F4 = C_BO + 4
N_CHUNKS = C_F4 + 3 * NJ

SLABS = [("gr", 0), ("gr", 1), ("q", 0), ("k", 0), ("v", 0), ("q", 1), ("k", 1), ("v", 1),
         ("xr", 0), ("xr", 1), ("ga", 0), ("ga", 1), ("gb", 0), ("gb", 1)]
COL0 = {"q": 0, "k": D, "v": 2 * D, "xr": 3 * D, "gr": 4 * D, "ga": 5 * D, "gb": 6 * D}
FM_SLABS = ("q", "k", "xr", "gr")
HEAD0 = 10
GATE0 = 20

N_NORMS = 11
PLAIN = (2, 10)
X_VERSION = [0, 1, 2, 3, 4, 5, 6, 6, 7, 8, 9]
TURN = {0: 0, "merge": 1, 1: 2, 3: 3, 4: 4, 5: 5, 6: 6, 7: 7, 8: 8, 9: 9}


def build(nc, d, out):
    ctx = ExitStack()
    with ctx:
        def sb(name, shape, dt=F32):
            return ctx.enter_context(nc.sbuf_tensor(name, shape, dt))

        def sem(name):
            return ctx.enter_context(nc.semaphore(name))

        ps = ctx.enter_context(nc.psum_tensor("ps", [P, 8, 512], F32))

        raw = sb("raw", [P, RING, CH])
        w_hi = sb("w_hi", [P, RING, CH], F32R)
        w_lo = sb("w_lo", [P, RING, CH], F32R)
        X = sb("X", [P, NH, D])
        xn = sb("xn", [P, NH, D])
        xT_hi = sb("xT_hi", [P, KD, S], F32R)
        xT_lo = sb("xT_lo", [P, KD, S], F32R)
        oT_hi = sb("oT_hi", [P, KD, S], F32R)
        oT_lo = sb("oT_lo", [P, KD, S], F32R)
        gain = sb("gain", [P, 2, D])
        ident = sb("ident", [P, P])
        ones = sb("ones", [P, P])
        later = sb("later", [P, P])
        before = sb("before", [P, P])
        par_rows = sb("par_rows", [P, P])
        par = sb("par", [P, P])
        half_b = sb("half_b", [P, 16])
        sp4 = sb("sp4", [P, 16])
        spt = sb("spt", [P, 6, 8])
        ss = sb("ss", [P, 2 * N_NORMS])
        var = sb("var", [P, 2 * N_NORMS])
        rstd = sb("rstd", [P, 2 * N_NORMS])
        minus_half = sb("minus_half", [P, 1])
        b_mrg = sb("b_mrg", [P, D])
        mem = sb("mem", [P, 18200])

        def view(at, *dims):
            n = 1
            for x in dims:
                n *= x
            v = mem[:, at:at + n]
            names = "abc"[:len(dims)]
            if len(dims) == 1:
                return v
            return v.rearrange("p (" + " ".join(names) + ") -> p " + " ".join(names),
                               **{names[i]: dims[i] for i in range(1, len(dims))})

        qk = view(0, 4, 1024)
        v_tm = view(4096, NH, D)
        gr = view(6144, KD, S)
        xrp = view(8192, KD, S + 3)
        xc = view(10272, KD, S)
        bias_t = view(12320, 3, 384)
        sbuf_s = view(13472, 2, 384)
        pT = view(14240, 2, 384)
        rg_t = view(15008, 3, S)
        w_bd = view(15776, 2, KD, P)
        th = xn[:, :, :].rearrange("p h d -> p (h d)").rearrange("p (t s) -> p t s", s=S)
        stat = sb("stat", [P, 2, 4])
        silu = view(0, NH, GW)
        h_tm = view(512, NH, GW)
        u_tm = view(0, NH, DA)
        g_tm = view(4096, NH, DA)
        ln_g = view(8192, DA)
        ln_b = view(10240, DA)
        ws_t = view(12288, NG, P)
        ws_r = view(13312, NG, P)
        uv = view(14336, 2, NH, GW)
        bn = sb("bn", [P, NH, 4, 6])
        mv = sb("mv", [P, NH, 2])
        ln_rs = sb("ln_rs", [P, NH, 2])
        q_b = view(0, KD, S)
        k_b = view(16384, 2, S)
        v_b = view(16384 + 512, NH, 256)
        z_abs = view(2048, 3, 512)
        z_sp = view(3584, 3, 512)
        z_ls = view(5120, 3, 512)
        z_a = view(6656, 3, 512)

        skew = nc.dram_tensor("skew", (HEADS, P * TAB), F32, kind="Internal").ap()

        s_skew = sem("s_skew")
        s_x = sem("s_x")
        s_gain = [sem("s_gain0"), sem("s_gain1")]
        s_raw = [sem(f"s_raw{i}") for i in range(RING)]
        s_hi = sem("s_hi")
        s_lo = sem("s_lo")
        s_mm = sem("s_mm")
        s_const = sem("s_const")
        s_par = sem("s_par")
        s_parT = sem("s_parT")
        s_parc = sem("s_parc")
        s_sp = sem("s_sp")
        s_spe = sem("s_spe")
        s_xup = sem("s_xup")
        s_sq = sem("s_sq")
        s_var = sem("s_var")
        s_rstd = sem("s_rstd")
        s_xn = sem("s_xn")
        s_turn = sem("s_turn")
        s_xhi = sem("s_xhi")
        s_xlo = sem("s_xlo")
        s_out = sem("s_out")
        s_slab = sem("s_slab")
        s_bsum = sem("s_bsum")
        s_bm = [sem("s_bm0"), sem("s_bm1")]
        s_bias = [sem(f"s_bias{i}") for i in range(3)]
        s_mask = sem("s_mask")
        s_sc = sem("s_sc")
        s_sb = sem("s_sb")
        s_max = sem("s_max")
        s_exp = sem("s_exp")
        s_rec = sem("s_rec")
        s_pn = sem("s_pn")
        s_pt = sem("s_pt")
        s_ptc = sem("s_ptc")
        s_pv = sem("s_pv")
        s_ohi = sem("s_ohi")
        s_olo = sem("s_olo")
        s_wbd = sem("s_wbd")
        s_z0 = sem("s_z0")
        s_cv = sem("s_cv")
        s_gt = sem("s_gt")
        s_ra = sem("s_ra")
        s_rd = sem("s_rd")
        s_sqrt = sem("s_sqrt")
        s_bx = sem("s_bx")
        s_scan = sem("s_scan")
        s_y = sem("s_y")
        s_yhi = sem("s_yhi")
        s_ylo = sem("s_ylo")
        s_mrg = sem("s_mrg")
        s_silu = sem("s_silu")
        s_h = sem("s_h")
        s_hT = sem("s_hT")
        s_hhi = sem("s_hhi")
        s_hlo = sem("s_hlo")
        s_ln = sem("s_ln")
        s_ws = sem("s_ws")
        s_wsm = sem("s_wsm")
        s_wsT = sem("s_wsT")
        s_wsc = sem("s_wsc")
        s_ge = sem("s_ge")
        s_bn = sem("s_bn")
        s_mv = sem("s_mv")
        s_lve = sem("s_lve")
        s_lrs = sem("s_lrs")
        s_lv = sem("s_lv")
        s_spa = sem("s_spa")
        s_uv = sem("s_uv")
        s_uvT = sem("s_uvT")
        s_uhi = sem("s_uhi")
        s_ulo = sem("s_ulo")
        s_kv = sem("s_kv")
        s_q = sem("s_q")
        s_z = sem("s_z")
        s_ab = sem("s_ab")
        s_ze = sem("s_ze")
        s_zl = sem("s_zl")
        s_zs = sem("s_zs")
        s_zm = sem("s_zm")
        s_ex = sem("s_ex")
        s_zd = sem("s_zd")
        s_za = sem("s_za")
        s_zam = sem("s_zam")
        s_zo = sem("s_zo")
        s_zhi = sem("s_zhi")
        s_zlo = sem("s_zlo")

        def acc(h, base=0):
            return ps[:, base + 2 * h:base + 2 * h + 2, :].rearrange("p b n -> p (b n)")

        def slab_banks(s):
            return 4 + 2 * (s % 2)

        def f32(ap):
            return ap.bitcast(F32)

        ffns = [(C_F0, 1, d["w_ffn_in"], d["w_ffn_out"])]
        for c0, n, i, s in ((C_F1, 3, 0, 0), (C_F2, 5, 0, 1), (C_F3, 7, 1, 0), (C_F4, 9, 1, 1)):
            ffns.append((c0, n, d["ffn_w_in_2"][i, s], d["ffn_w_out_2"][i, s]))

        gains = [d["norm_mix_g"], d["norm_ffn_g"], d["final_norm_g"], d["ffn_norm_2"][0, 0],
                 d["mix_norm_2"][0], d["ffn_norm_2"][0, 1], d["kv_norm_2"], d["ffn_norm_2"][1, 0],
                 d["mix_norm_2"][1], d["ffn_norm_2"][1, 1], d["final_norm_2"]]

        block = ctx.enter_context(nc.Block())

        @block.sync
        def _(sp):
            def room(c):
                if not isinstance(c, int) or c >= RING:
                    sp.wait_ge(s_lo, c - (RING - 1))

            def send(slot, dst, src):
                sp.dma_start(dst, src).then_inc(s_raw[slot], 16)

            def load_cols(c, w, k0, col, slot):
                room(c)
                dst = raw[:, slot, :].rearrange("p (k n) -> p k n", k=4)
                src = w.rearrange("(k p) n -> p k n", p=P)
                for i in range(2):
                    send(slot, dst[:, 2 * i:2 * i + 2, :],
                         src[:, k0 + 2 * i:k0 + 2 * i + 2, col:col + 512])

            def load_rows(c, w, k0, slot):
                room(c)
                dst = raw[:, slot, :].rearrange("p (k n) -> p k n", k=2)
                src = w.rearrange("(k p) n -> p k n", p=P)
                for i in range(2):
                    send(slot, dst[:, i:i + 1, :], src[:, bass.ds(k0 + i, 1), :])

            def load_gate_up(c, w, a, j, slot):
                room(c)
                dst = raw[:, slot, :].rearrange("p (k g n) -> p k g n", k=4, g=2)
                src = w.rearrange("(k p) (g n) -> g p k n", p=P, g=2)
                for g in range(2):
                    send(slot, dst[:, :, g, :], src[g, :, 4 * a:4 * a + 4, bass.ds(j * GW, GW)])

            def feed_forward(c0, w_up, w_down):
                for j in range(2):
                    for a in range(2):
                        load_gate_up(c0 + 2 * j + a, w_up, a, j, (c0 + 2 * j + a) % RING)
                load_rows(c0 + 4, w_down, 0, (c0 + 4) % RING)
                with sp.Fori(0, NJ - 2) as i:
                    for a in range(2):
                        load_gate_up(i * 3 + (c0 + 5 + a), w_up, a, i + 2, (c0 + 5 + a) % RING)
                    load_rows(i * 3 + (c0 + 7), w_down, i * 2 + 2, (c0 + 7) % RING)
                load_rows(c0 + 3 * NJ - 1, w_down, 2 * NJ - 2, (c0 + 3 * NJ - 1) % RING)

            for h in range(NH):
                sp.dma_start(X[:, h, :], d["x"][h * P:(h + 1) * P, :]).then_inc(s_x, 16)
            for s, (kind, n) in enumerate(SLABS):
                for a in range(2):
                    c = 2 * s + a
                    load_cols(c, d["w_in"], 4 * a, COL0[kind] + 512 * n, c % RING)
            for c0, w in ((C_AO, d["w_attn_out"]), (C_RO, d["w_rnn_out"]), (C_WO, d["w_o"])):
                for i in range(4):
                    load_rows(c0 + i, w, 2 * i, (c0 + i) % RING)
            feed_forward(ffns[0][0], ffns[0][2], ffns[0][3])
            feed_forward(ffns[1][0], ffns[1][2], ffns[1][3])
            for s in range(8):
                for a in range(2):
                    c = C_AI + 2 * s + a
                    load_cols(c, d["a_w_in_2"], 4 * a, (512 * s + DA) % (2 * DA), c % RING)
            for i in range(8):
                load_rows(C_AW + i, d["a_w_out_2"], 2 * i, (C_AW + i) % RING)
            feed_forward(ffns[2][0], ffns[2][2], ffns[2][3])
            for a in range(2):
                load_cols(C_KV + a, d["w_kv_2"], 4 * a, 0, (C_KV + a) % RING)
            feed_forward(ffns[3][0], ffns[3][2], ffns[3][3])
            for s in range(2):
                for a in range(2):
                    c = C_Q + 2 * s + a
                    load_cols(c, d["b_w_q_2"], 4 * a, 512 * s, c % RING)
            wo = d["b_w_o_2"].rearrange("(s k g e) n -> s k e g n", s=2, k=2, g=GRP)
            for i in range(4):
                c = C_BO + i
                room(c)
                dst = raw[:, c % RING, :].rearrange("p (g n) -> p g n", g=2)
                for k in range(2):
                    send(c % RING, dst[k * HD:(k + 1) * HD, :, :],
                         wo[i // 2, k, :, 2 * (i % 2):2 * (i % 2) + 2, :])
            feed_forward(ffns[4][0], ffns[4][2], ffns[4][3])
            for h in range(NH):
                sp.wait_ge(s_xn, 2 * N_NORMS - 1 + h)
                sp.dma_start(out[h * P:(h + 1) * P, :], xn[:, h, :]).then_inc(s_out, 16)
            sp.wait_ge(s_out, 32)

        @block.gpsimd
        def _(pool):
            def gain_load(n):
                if n >= 2:
                    if n - 2 == 2:
                        pool.wait_ge(s_xup, XUP[3] + 2)
                    else:
                        pool.wait_ge(s_xn, XN_AT[n - 2] + 2)
                pool.dma_start(gain[:, n % 2, :], gains[n].rearrange("(o n) -> o n", o=1)
                               .broadcast_to([P, D])).then_inc(s_gain[n % 2], 16)

            def norm(n):
                for h in range(NH):
                    i = 2 * n + h
                    pool.wait_ge(s_sq, i + 1)
                    pool.tensor_scalar(var[:, i:i + 1], ss[:, i:i + 1], 1.0 / D, EPS,
                                       ALU.mult, ALU.add).then_inc(s_var, 1)
                    pool.wait_ge(s_var, i + 1)
                    pool.tensor_tensor(rstd[:, i:i + 1], var[:, i:i + 1], minus_half[:, :],
                                       ALU.pow).then_inc(s_rstd, 1)

            pool.memset(par_rows[:, :], 0.0).then_inc(s_z0, 1)
            pool.wait_ge(s_z0, 1)
            rows = [(d["conv_w"].rearrange("j (t p) -> (j t) p", p=P), 0, 32)]
            for r, name in ((32, "conv_b"), (40, "b_rg_r"), (48, "b_rg_i"), (56, "rg_lambda")):
                rows.append((d[name].rearrange("(t p) -> t p", p=P), r, 8))
            rows.append((d["a_b_s_2"], 64, 8))
            for src, r, n in rows:
                pool.dma_start(par_rows[r:r + n, :], src).then_inc(s_par, 16)
            gain_load(0)
            gain_load(1)
            pool.memset(minus_half[:, :], -0.5).then_inc(s_const, 1)
            pool.memset(ident[:, :], 0.0).then_inc(s_const, 1)
            pool.memset(ones[:, :], 1.0).then_inc(s_const, 1)
            pool.wait_ge(s_const, 3)
            pool.affine_select(out=ident[:, :], in_=ident[:, :], compare_op=ALU.not_equal, fill=1.0,
                               base=0, pattern=[[-1, P]], channel_multiplier=1).then_inc(s_const, 1)
            pool.affine_select(out=later[:, :], in_=ones[:, :], compare_op=ALU.is_gt, fill=0.0,
                               base=0, pattern=[[-1, P]], channel_multiplier=1).then_inc(s_const, 1)
            pool.affine_select(out=before[:, :], in_=ones[:, :], compare_op=ALU.is_gt, fill=0.0,
                               base=0, pattern=[[1, P]], channel_multiplier=-1).then_inc(s_const, 1)
            norm(0)
            pool.memset(mem[:, 15776:15776 + 2048], 0.0).then_inc(s_z0, 1)
            pool.memset(xrp[:, :, 0:3], 0.0).then_inc(s_z0, 1)
            pool.wait_ge(s_z0, 3)
            for g, name in enumerate(("w_rg_r", "w_rg_i")):
                src = d[name].rearrange("(t b) i o -> b i t o", b=2)
                for b in range(2):
                    pool.dma_start(w_bd[b * HD:(b + 1) * HD, g, :, b * HD:(b + 1) * HD],
                                   src[b]).then_inc(s_wbd, 16)
            def merge_bias(s):
                pool.dma_start(b_mrg[:, (s % 2) * 512:(s % 2 + 1) * 512],
                               d["b_merge"][(s - 10) * 512:(s - 9) * 512]
                               .rearrange("(o n) -> o n", o=1).broadcast_to([P, 512])
                               ).then_inc(s_bm[s % 2], 16)

            merge_bias(10)
            merge_bias(11)
            pool.dma_start(skew.rearrange("i (q n) -> i q n", n=TAB),
                           d["rel_rev"].rearrange("i (o n) -> i o n", o=1)
                           .broadcast_to([HEADS, P, TAB])).then_inc(s_skew, 16)
            pool.wait_ge(s_skew, 16)
            for i in range(HEADS):
                if i >= 3:
                    pool.wait_ge(s_sb, i - 2)
                slot = bias_t[:, i % 3, :]
                for off, c0, n in ((128, 0, 128), (0, 128, 256)):
                    src = skew[i, 0:P * (TAB - 1)].rearrange(
                        "(q n) -> q n", n=TAB - 1)[:, P - 1 + off:P - 1 + off + n]
                    pool.dma_start(slot[:, c0:c0 + n], src).then_inc(s_bias[i % 3], 16)
                pool.wait_ge(s_bias[i % 3], 32 * (i // 3 + 1))
                pool.memset(bias_t[0:64, i % 3, 64:128], NEG)
                pool.memset(bias_t[0:64, i % 3, 320:384], NEG).then_inc(s_mask, 1)
            for s in (12, 13):
                pool.wait_ge(s_bsum, 2 * (s - 11))
                merge_bias(s)
            for n in (1, 2, 3):
                gain_load(n + 1)
                norm(n)
            pool.wait_ge(s_xup, XUP[2])
            pool.dma_start(ln_g, d["a_ln_g_2"].rearrange("(o n) -> o n", o=1).broadcast_to([P, DA])
                           ).then_inc(s_ln, 16)
            pool.dma_start(ln_b, d["a_ln_b_2"].rearrange("(o n) -> o n", o=1).broadcast_to([P, DA])
                           ).then_inc(s_ln, 16)
            pool.dma_start(ws_r, d["a_w_s_2"].rearrange("g t s -> t g s")).then_inc(s_ws, 16)
            pool.wait_ge(s_ws, 16)
            pool.affine_select(out=ws_r, in_=ws_r, compare_op=ALU.is_ge, fill=0.0, base=0,
                               pattern=[[0, NG], [-1, P]], channel_multiplier=1).then_inc(s_wsm, 1)
            gain_load(5)
            norm(4)
            for h in range(NH):
                pool.wait_ge(s_mv, h + 1)
                pool.tensor_scalar(ln_rs[:, h, 0:1], mv[:, h, 1:2], 1.0, LN_EPS,
                                   ALU.mult, ALU.add).then_inc(s_lve, 1)
                pool.wait_ge(s_lve, h + 1)
                pool.tensor_tensor(ln_rs[:, h, 1:2], ln_rs[:, h, 0:1], minus_half[:, :],
                                   ALU.pow).then_inc(s_lrs, 1)
            for n in range(5, N_NORMS):
                if n + 1 < N_NORMS:
                    gain_load(n + 1)
                norm(n)

        @block.tensor
        def _(pe):
            def product(dst, x, w, start, stop):
                pe.matmul(dst, x[0], w[0], start=start, stop=False, skip_group_check=True)
                pe.matmul(dst, x[0], w[1], start=False, stop=False, skip_group_check=True)
                return pe.matmul(dst, x[1], w[0], start=False, stop=stop, skip_group_check=True)

            def both(t, *index):
                return [x[index] for x in t]

            ALL = slice(None)
            XT = (xT_hi, xT_lo)
            OT = (oT_hi, oT_lo)

            def slot(c0, k):
                return [w[:, c0 % RING, :].rearrange("p (k n) -> p k n", k=k) for w in (w_hi, w_lo)]

            def split(c):
                pe.wait_ge(s_lo, c + 1)

            def tm_cols(c0, a, banks, turn=None):
                w = slot(c0, 4)
                for h in range(NH):
                    if turn is not None:
                        pe.wait_ge(s_xlo, 4 * turn + 2 * h + a + 1)
                    for k in range(4):
                        m = product(ps[:, banks + h, :],
                                    both(XT, ALL, 4 * a + k, slice(h * P, (h + 1) * P)),
                                    both(w, ALL, k, ALL), a == 0 and k == 0, a == 1 and k == 3)
                    m.then_inc(s_mm, 1)

            def fm_cols(c0, a, banks, turn=None):
                w = slot(c0, 4)
                if turn is not None:
                    pe.wait_ge(s_xlo, 4 * turn + 2 + a + 1)
                for t in range(4):
                    for k in range(4):
                        cols = both(w, ALL, k, slice(t * P, (t + 1) * P))
                        x = both(XT, ALL, 4 * a + k, ALL)
                        dst = ps[:, banks + t // 2, (t % 2) * S:(t % 2 + 1) * S]
                        m = product(dst, cols, x, a == 0 and k == 0 and t % 2 == 0,
                                    a == 1 and k == 3)
                    if t % 2:
                        m.then_inc(s_mm, 1)

            def tm_rows(c0, src, k0, base, start, stop):
                w = slot(c0, 2)
                for h in range(NH):
                    for n in range(2):
                        for k in range(2):
                            m = product(ps[:, base + 2 * h + n, :],
                                        both(src, ALL, k0 + k, slice(h * P, (h + 1) * P)),
                                        both(w, ALL, k, slice(n * 512, (n + 1) * 512)),
                                        start and k == 0, stop and k == 1)
                    m.then_inc(s_mm, 1)

            def turn_xn(i, xn_at):
                for h in range(NH):
                    pe.wait_ge(s_xn, xn_at + h + 1)
                    for k in range(KD):
                        m = pe.transpose(acc(h)[:, k * P:(k + 1) * P],
                                         xn[:, h, k * P:(k + 1) * P], ident[:, :])
                        if k % 4 == 3:
                            m.then_inc(s_turn, 1)

            def feed_forward(f, c0, n):
                def up(c, slot_of, a, first=False):
                    split(c)
                    tm_cols(slot_of, a, 4, TURN[n] if first else None)

                def turn_h(j):
                    pe.wait_ge(s_h, j * 2 + 2)
                    for h in range(NH):
                        for t in range(2):
                            m = pe.transpose(ps[:, 6, t * S + h * P:t * S + (h + 1) * P],
                                             h_tm[:, h, t * P:(t + 1) * P], ident[:, :])
                    m.then_inc(s_hT, 1)

                def down(c, slot_of, j, start, stop):
                    split(c)
                    pe.wait_ge(s_hlo, j + 1)
                    tm_rows(slot_of, OT, 0, 0, start, stop)

                j0 = f * NJ
                for a in range(2):
                    up(c0 + a, c0 + a, a, True)
                pe.wait_ge(s_h, 2 * j0 + 2)
                up(c0 + 2, c0 + 2, 0)
                turn_h(j0)
                up(c0 + 3, c0 + 3, 1)
                down(c0 + 4, c0 + 4, j0, True, False)
                with pe.Fori(0, NJ - 2) as i:
                    pe.wait_ge(s_h, i * 2 + (2 * j0 + 4))
                    up(i * 3 + (c0 + 5), c0 + 5, 0)
                    turn_h(i + (j0 + 1))
                    up(i * 3 + (c0 + 6), c0 + 6, 1)
                    down(i * 3 + (c0 + 7), c0 + 7, i + (j0 + 1), False, False)
                turn_h(j0 + NJ - 1)
                down(c0 + 3 * NJ - 1, c0 + 3 * NJ - 1, j0 + NJ - 1, False, True)

            pe.wait_ge(s_const, 6)
            pe.wait_ge(s_par, 96)
            pe.transpose(ps[:, 7, 0:P], par_rows[:, :], ident[:, :]).then_inc(s_parT, 1)
            turn_xn(0, 0)

            def scores(i):
                q = qk[:, 2 * (i // 8), :].rearrange("p (t s) -> p t s", s=S)
                k = qk[:, 2 * (i // 8) + 1, :].rearrange("p (t s) -> p t s", s=S)
                rows = slice(HD * (i % 2), HD * (i % 2) + HD)
                t = (i % 8) // 2
                pe.wait_ge(s_slab, SLAB_AT["k", i // 8])
                if i >= 2:
                    pe.wait_ge(s_ptc, i - 1)
                pe.matmul(ps[:, i % 2, 0:P], q[rows, t, 0:P], k[rows, t, 0:P], start=True, stop=True)
                pe.matmul(ps[:, i % 2, P:P + S], q[rows, t, P:S], k[rows, t, :],
                          start=True, stop=True).then_inc(s_sc, 1)

            def turn_p(i):
                pe.wait_ge(s_pn, 2 * i + 2)
                for n in range(3):
                    m = pe.transpose(ps[:, i % 2, n * P:(n + 1) * P],
                                     sbuf_s[:, i % 2, n * P:(n + 1) * P], ident[:, :])
                m.then_inc(s_pt, 1)

            def pv(i):
                pe.wait_ge(s_ptc, i + 1)
                pe.wait_ge(s_slab, SLAB_AT["v", i // 8])
                t = i // 2
                if i % 2 == 0 and t >= 1:
                    pe.wait_ge(s_olo, t)
                o = ps[HD * (i % 2):HD * (i % 2) + HD, 3, 0:S]
                val = [v_tm[:, h, i * HD:(i + 1) * HD] for h in range(NH)]
                pe.matmul(o[:, 0:P], val[0], pT[:, i % 2, 0:P], start=True, stop=True)
                pe.matmul(o[:, P:S], val[0], pT[:, i % 2, P:S], start=True, stop=False)
                pe.matmul(o[:, P:S], val[1], pT[:, i % 2, S:S + P], start=False,
                          stop=True).then_inc(s_pv, 1)

            def gates(t):
                if t == 0:
                    pe.wait_ge(s_wbd, 64)
                pe.wait_ge(s_cv, 4 * t + 4)
                if t >= 1:
                    pe.wait_ge(s_ra, 4 * t - 2)
                for g in range(2):
                    m = pe.matmul(ps[:, 2, g * S:(g + 1) * S], w_bd[:, g, t, :], xc[:, t, :],
                                  start=True, stop=True)
                m.then_inc(s_gt, 1)

            for c in range(28):
                i, t = c - HEAD0, c - GATE0
                if 0 <= i < HEADS:
                    scores(i)
                if 1 <= i <= HEADS:
                    turn_p(i - 1)
                if 0 <= t < KD:
                    gates(t)
                s, a = c // 2, c % 2
                split(c)
                if a == 0 and s >= 2:
                    pe.wait_ge(s_slab, 2 * (s - 1))
                turn = TURN[0] if s == 0 else None
                if s == 1 and a == 0:
                    pe.wait_ge(s_parc, 1)
                if SLABS[s][0] in FM_SLABS:
                    fm_cols(c, a, slab_banks(s), turn)
                else:
                    tm_cols(c, a, slab_banks(s), turn)
                if 1 <= i <= HEADS:
                    pv(i - 1)

            for n in range(4):
                split(C_AO + n)
                pe.wait_ge(s_olo, KD)
                pe.wait_ge(s_ra, 4 * KD - 2)
                pe.wait_ge(s_ptc, HEADS)
                tm_rows(C_AO + n, OT, 2 * n, 0, n == 0, n == 3)
            for n in range(4):
                split(C_RO + n)
                if n == 0:
                    pe.wait_ge(s_slab, 28)
                pe.wait_ge(s_ylo, 2)
                tm_rows(C_RO + n, XT, 2 * n, 4, n == 0, n == 3)
            turn_xn(TURN["merge"], 2)
            for n in range(4):
                split(C_WO + n)
                pe.wait_ge(s_xlo, 4 * TURN["merge"] + 4)
                tm_rows(C_WO + n, XT, 2 * n, 4, n == 0, n == 3)

            turn_xn(TURN[1], XN_AT[1])
            feed_forward(0, ffns[0][0], 1)
            turn_xn(TURN[3], XN_AT[3])
            feed_forward(1, ffns[1][0], 3)

            pe.wait_ge(s_wsm, 1)
            for g in range(NG):
                m = pe.transpose(ps[:, 4 + g // 4, (g % 4) * P:(g % 4 + 1) * P], ws_r[:, g, :],
                                 ident[:, :])
            m.then_inc(s_wsT, 1)
            turn_xn(TURN[4], XN_AT[4])
            for s in range(8):
                for a in range(2):
                    c = C_AI + 2 * s + a
                    split(c)
                    if a == 0 and s == 0:
                        pe.wait_ge(s_wsc, 1)
                    if a == 0 and s >= 2:
                        pe.wait_ge(s_ge, 2 * (s - 1))
                    tm_cols(c, a, slab_banks(s), TURN[4] if s == 0 else None)

            def spatial(g):
                pe.wait_ge(s_lv, 6)
                pe.wait_ge(s_ge, 16)
                if g >= 2:
                    pe.wait_ge(s_uv, 2 * (g - 1))
                for h in range(NH):
                    m = pe.matmul(ps[:, 4 + g % 2, h * GW:(h + 1) * GW], ws_t[:, g, :],
                                  g_tm[:, h, g * GW:(g + 1) * GW], start=True, stop=True)
                m.then_inc(s_spa, 1)

            def turn_uv(g):
                pe.wait_ge(s_uv, 2 * g + 2)
                if g >= 2:
                    pe.wait_ge(s_ulo, g - 1)
                for h in range(NH):
                    for t in range(2):
                        m = pe.transpose(ps[:, 6 + g % 2, t * S + h * P:t * S + (h + 1) * P],
                                         uv[:, g % 2, h, t * P:(t + 1) * P], ident[:, :])
                m.then_inc(s_uvT, 1)

            spatial(0)
            spatial(1)
            turn_uv(0)
            for g in range(NG):
                if g + 2 < NG:
                    spatial(g + 2)
                if g + 1 < NG:
                    turn_uv(g + 1)
                split(C_AW + g)
                pe.wait_ge(s_ulo, g + 1)
                tm_rows(C_AW + g, OT, 2 * (g % 2), 0, g == 0, g == NG - 1)

            turn_xn(TURN[5], XN_AT[5])
            feed_forward(2, ffns[2][0], 5)

            turn_xn(TURN[6], XN_AT[6])
            for a in range(2):
                c = C_KV + a
                split(c)
                pe.wait_ge(s_xlo, 4 * TURN[6] + 2 + a + 1)
                w = slot(c, 4)
                for t in range(2):
                    for k in range(4):
                        m = product(ps[:, 4, t * S:(t + 1) * S],
                                    both(w, ALL, k, slice(t * P, (t + 1) * P)),
                                    both(XT, ALL, 4 * a + k, ALL),
                                    a == 0 and k == 0 and t == 0, a == 1 and k == 3)
                m.then_inc(s_mm, 1)
                for h in range(NH):
                    for k in range(4):
                        m = product(ps[:, 5, h * 256:(h + 1) * 256],
                                    both(XT, ALL, 4 * a + k, slice(h * P, (h + 1) * P)),
                                    both(w, ALL, k, slice(256, 512)),
                                    a == 0 and k == 0 and h == 0, a == 1 and k == 3)
                m.then_inc(s_mm, 1)

            turn_xn(TURN[7], XN_AT[7])
            pe.wait_ge(s_kv, 2)
            feed_forward(3, ffns[3][0], 7)

            turn_xn(TURN[8], XN_AT[8])
            for s in range(2):
                for a in range(2):
                    split(C_Q + 2 * s + a)
                    fm_cols(C_Q + 2 * s + a, a, slab_banks(s), TURN[8] if s == 0 else None)

            BLOCKS = ((0, 0), (0, 1), (1, 1))

            def logits(j):
                rows = slice(HD * (j % 2), HD * (j % 2) + HD)
                pe.wait_ge(s_q, 4)
                if j >= 1:
                    pe.wait_ge(s_zs, 2 * j)
                for b, (sh, th_) in enumerate(BLOCKS):
                    q = q_b[rows, 4 * (j // 2):4 * (j // 2) + 4, th_ * P:(th_ + 1) * P]
                    m = pe.matmul(ps[:, b, :], k_b[rows, j // 2, sh * P:(sh + 1) * P], q,
                                  start=True, stop=True)
                m.then_inc(s_z, 1)

            def sums(j):
                pe.wait_ge(s_zm, 2 * j + 2)
                if j >= 1:
                    pe.wait_ge(s_zd, j)
                else:
                    pe.wait_ge(s_q, 4)
                pe.matmul(ps[:, 3, :], later[:, :], z_sp[:, 0, :], start=True, stop=True)
                pe.matmul(ps[:, 4, :], later[:, :], z_sp[:, 1, :], start=True, stop=False)
                pe.matmul(ps[:, 4, :], ones[:, :], z_sp[:, 2, :], start=False, stop=True)
                pe.matmul(ps[:, 5, :], later[:, :], z_sp[:, 2, :], start=True,
                          stop=True).then_inc(s_ex, 1)

            def weigh(j):
                pe.wait_ge(s_zam, 2 * j + 2)
                if j >= 2 and j % 2 == 0:
                    pe.wait_ge(s_zlo, j // 2)
                rows = slice(HD * (j % 2), HD * (j % 2) + HD)
                v = [v_b[:, h, j * HD:(j + 1) * HD] for h in range(NH)]
                pe.matmul(ps[rows, 6, :], v[0], z_a[:, 0, :], start=True, stop=True)
                pe.matmul(ps[rows, 7, :], v[0], z_a[:, 1, :], start=True, stop=False)
                pe.matmul(ps[rows, 7, :], v[1], z_a[:, 2, :], start=False, stop=True).then_inc(s_zo, 1)

            logits(0)
            for j in range(NKV):
                if j + 1 < NKV:
                    logits(j + 1)
                sums(j)
                weigh(j)

            for n in range(4):
                split(C_BO + n)
                pe.wait_ge(s_zlo, 2)
                tm_rows(C_BO + n, OT, 2 * n, 0, n == 0, n == 3)
            turn_xn(TURN[9], XN_AT[9])
            feed_forward(4, ffns[4][0], 9)

        @block.scalar
        def _(act):
            def hi(c, slot=None):
                slot = c % RING if slot is None else slot
                if isinstance(c, int):
                    if c >= N_CHUNKS:
                        return
                    act.wait_ge(s_raw[slot], 32 * (c // RING + 1))
                    if c >= RING:
                        act.wait_ge(s_mm, 2 * (c - RING) + 2)
                act.activation(w_hi[:, slot, :], raw[:, slot, :], ACT.Copy).then_inc(s_hi, 1)

            def squares(n, version):
                for h in range(NH):
                    if version == 0:
                        act.wait_ge(s_x, 32)
                    else:
                        act.wait_ge(s_xup, XUP[version] + h + 1)
                    act.activation(xn[:, h, :], X[:, h, :], ACT.Square,
                                   accum_out=ss[:, 2 * n + h:2 * n + h + 1]).then_inc(s_sq, 1)

            def turned(i, used=None):
                if used is not None:
                    act.wait_ge(s_mm, 2 * used + 2)
                for h in range(NH):
                    for g in range(2):
                        act.wait_ge(s_turn, 4 * i + 2 * h + g + 1)
                        act.activation(xT_hi[:, 4 * g:4 * g + 4, h * P:(h + 1) * P],
                                       ps[:, 2 * h + g, :].rearrange("p (k n) -> p k n", k=4),
                                       ACT.Copy).then_inc(s_xhi, 1)

            def feed_forward(f, c0):
                j0 = f * NJ

                def h_hi(j):
                    act.wait_ge(s_hT, j + 1)
                    act.activation(oT_hi[:, 0:2, :], ps[:, 6, :].rearrange("p (t s) -> p t s", t=2),
                                   ACT.Copy).then_inc(s_hhi, 1)

                def gate(c, j):
                    for h in range(NH):
                        act.wait_ge(s_mm, c * 2 + (h + 1))
                        act.activation(silu[:, h, :], ps[:, 4 + h, 0:GW], ACT.Silu).then_inc(s_silu, 1)

                def next_hi(n, i):
                    slot = (c0 + n) % RING
                    if isinstance(i, int):
                        hi(c0 + n + 3 * i + RING)
                        return
                    act.wait_ge(s_raw[slot], i * 32 + 32 * ((c0 + n + RING) // RING + 1))
                    act.wait_ge(s_mm, i * 6 + (2 * (c0 + n) + 2))
                    hi(i, slot)

                hi(c0 + 3)
                gate(c0 + 1, j0)
                hi(c0 + 4)
                h_hi(j0)
                hi(c0 + 5)
                gate(c0 + 3, j0 + 1)
                hi(c0 + 6)
                hi(c0 + 7)
                def step(i):
                    h_hi(i + (j0 + 1))
                    next_hi(5, i)
                    gate(i * 3 + (c0 + 6), i + (j0 + 2))
                    next_hi(6, i)
                    next_hi(7, i)

                last = c0 == C_F4
                with act.Fori(0, NJ - 2 - last) as i:
                    step(i)
                if last:
                    step(NJ - 3)
                h_hi(j0 + NJ - 1)

            act.preload_act_table_set("exp_and_others")
            squares(0, 0)
            hi(0)
            turned(TURN[0])
            hi(1)
            hi(2)
            act.wait_ge(s_sp, 1)
            act.activation(spt[:, 1, :], spt[:, 0, :], ACT.Exp, scale=-1.0).then_inc(s_spe, 1)

            def band_exp(i):
                act.wait_ge(s_max, 2 * i + 2)
                for h, (c0, n) in enumerate(((0, P), (P, S))):
                    act.activation(sbuf_s[:, i % 2, c0:c0 + n], sbuf_s[:, i % 2, c0:c0 + n], ACT.Exp,
                                   bias=stat[:, i % 2, h:h + 1],
                                   accum_out=stat[:, i % 2, 2 + h:3 + h]).then_inc(s_exp, 1)

            def copy_p(i):
                act.wait_ge(s_pt, i + 1)
                act.activation(pT[:, i % 2, :], ps[:, i % 2, 0:384], ACT.Copy).then_inc(s_ptc, 1)

            def o_hi(t):
                act.wait_ge(s_pv, 2 * t + 2)
                act.activation(oT_hi[:, t, :], ps[:, 3, 0:S],
                               ACT.Copy).then_inc(s_ohi, 1)

            def gate_functions(t):
                act.wait_ge(s_gt, t + 1)
                if t == 0:
                    act.wait_ge(s_sp, SP_DONE)
                if t >= 1:
                    act.wait_ge(s_rd, 3 * t)
                for g in range(2):
                    act.activation(rg_t[:, g, :], ps[:, 2, g * S:(g + 1) * S], ACT.Tanh, scale=0.5,
                                   bias=half_b[:, 8 * g + t:8 * g + t + 1]).then_inc(s_ra, 1)
                act.wait_ge(s_ra, 4 * t + 2)
                act.activation(xrp[:, t, 3:3 + S], rg_t[:, 0, :], ACT.Exp, scale=sp4[:, 8 + t:9 + t],
                               bias=sp4[:, 8 + t:9 + t]).then_inc(s_ra, 1)
                act.activation(th[:, t, :], rg_t[:, 0, :], ACT.Tanh, scale=sp4[:, t:t + 1],
                               bias=sp4[:, t:t + 1]).then_inc(s_ra, 1)

            for c in range(28):
                i, t = c - HEAD0, c - GATE0
                if 1 <= i <= HEADS:
                    copy_p(i - 1)
                if 0 <= i < HEADS:
                    band_exp(i)
                if 0 <= t < KD:
                    gate_functions(t)
                if c % 2:
                    s = c // 2
                    kind, n = SLABS[s]
                    banks = slab_banks(s)
                    for h in range(NH):
                        src = ps[:, banks + h, :]
                        if kind in ("ga", "gb"):
                            act.wait_ge(s_bsum, 2 * (s - 10) + h + 1)
                            dst = qk[:, s - 10, h * 512:(h + 1) * 512]
                            act.activation(dst, dst, ACT.Tanh, scale=0.5).then_inc(s_slab, 1)
                            continue
                        act.wait_ge(s_mm, 2 * c + h + 1)
                        if kind == "xr":
                            act.wait_ge(s_z0, 3)
                            act.activation(xrp[:, 4 * n + 2 * h:4 * n + 2 * h + 2, 3:3 + S],
                                           src.rearrange("p (t s) -> p t s", t=2),
                                           ACT.Copy).then_inc(s_slab, 1)
                            continue
                        if kind == "gr":
                            dst = gr[:, 4 * n + 2 * h:4 * n + 2 * h + 2, :].rearrange("p t s -> p (t s)")
                        elif kind == "v":
                            dst = v_tm[:, h, n * 512:(n + 1) * 512]
                        else:
                            dst = qk[:, 2 * n + (kind == "k"), h * 512:(h + 1) * 512]
                        fn = ACT.Gelu_apprx_tanh if kind == "gr" else ACT.Copy
                        act.activation(dst, src, fn).then_inc(s_slab, 1)
                hi(c + RING)
                if 1 <= i <= HEADS and (i - 1) % 2:
                    o_hi((i - 1) // 2)

            act.wait_ge(s_rd, 3 * KD)
            act.activation(th[:, :, :], th[:, :, :], ACT.Sqrt, scale=0.25).then_inc(s_sqrt, 1)
            for n in range(4):
                if n == 0:
                    hi(C_AO + n + RING)
                    act.wait_ge(s_mm, 2 * C_AO)
                    for h in range(2):
                        act.wait_ge(s_y, h + 1)
                        act.activation(xT_hi[:, 4 * h:4 * h + 4, :], xc[:, 4 * h:4 * h + 4, :],
                                       ACT.Copy).then_inc(s_yhi, 1)
                else:
                    hi(C_AO + n + RING)
            for n in range(4):
                hi(C_RO + n + RING)
            turned(TURN["merge"], C_WO - 1)
            for n in range(4):
                hi(C_WO + n + RING)

            squares(1, 1)
            turned(TURN[1], C_F0 - 1)
            feed_forward(0, ffns[0][0])
            squares(2, 2)
            squares(3, 3)
            turned(TURN[3], C_F1 - 1)
            hi(C_F1 + 2)
            feed_forward(1, ffns[1][0])

            act.wait_ge(s_wsT, 1)
            act.activation(ws_t, ps[:, 4:6, :].rearrange("p b (g s) -> p (b g) s", s=P),
                           ACT.Copy).then_inc(s_wsc, 1)
            squares(4, 4)
            turned(TURN[4], C_AI - 1)
            hi(C_AI + 2)
            for s in range(8):
                for a in range(2):
                    c = C_AI + 2 * s + a
                    if a:
                        for h in range(NH):
                            act.wait_ge(s_mm, 2 * c + h + 1)
                            dst = g_tm if s < 4 else u_tm
                            act.activation(dst[:, h, 512 * (s % 4):512 * (s % 4 + 1)],
                                           ps[:, slab_banks(s) + h, :],
                                           ACT.Gelu_apprx_tanh).then_inc(s_ge, 1)
                    hi(c + RING)

            def uv_hi(g):
                act.wait_ge(s_uvT, g + 1)
                if g >= 2:
                    act.wait_ge(s_mm, 2 * (C_AW + g - 2) + 2)
                act.activation(oT_hi[:, 2 * (g % 2):2 * (g % 2) + 2, :],
                               ps[:, 6 + g % 2, :].rearrange("p (t s) -> p t s", t=2),
                               ACT.Copy).then_inc(s_uhi, 1)

            uv_hi(0)
            for g in range(NG):
                if g + 1 < NG:
                    uv_hi(g + 1)
                hi(C_AW + g + RING)
            squares(5, 5)
            turned(TURN[5], C_F2 - 1)
            feed_forward(2, ffns[2][0])

            squares(6, 6)
            turned(TURN[6], C_KV - 1)
            hi(C_KV + 2)
            act.wait_ge(s_mm, 2 * (C_KV + 1) + 1)
            act.activation(k_b, ps[:, 4, :].rearrange("p (t s) -> p t s", t=2),
                           ACT.Copy).then_inc(s_kv, 1)
            act.wait_ge(s_mm, 2 * (C_KV + 1) + 2)
            act.activation(v_b, ps[:, 5, :].rearrange("p (t s) -> p t s", t=2),
                           ACT.Copy).then_inc(s_kv, 1)
            hi(C_KV + 3)
            hi(C_KV + 4)
            squares(7, 6)
            turned(TURN[7], C_F3 - 1)
            feed_forward(3, ffns[3][0])

            squares(8, 7)
            turned(TURN[8], C_Q - 1)
            hi(C_Q + 2)
            for s in range(2):
                for a in range(2):
                    c = C_Q + 2 * s + a
                    if a:
                        for h in range(2):
                            act.wait_ge(s_mm, 2 * c + h + 1)
                            act.activation(q_b[:, 4 * s + 2 * h:4 * s + 2 * h + 2, :],
                                           ps[:, slab_banks(s) + h, :].rearrange("p (t s) -> p t s", t=2),
                                           ACT.Copy, scale=HD ** -0.5).then_inc(s_q, 1)
                    hi(c + RING)

            act.preload_act_table_set("natural_log_exp_and_others")

            def softplus_parts(j):
                act.wait_ge(s_z, j + 1)
                act.activation(z_abs, ps[:, 0:3, :], ACT.Abs).then_inc(s_ab, 1)
                act.wait_ge(s_ab, j + 1)
                act.activation(z_abs, z_abs, ACT.Exp, scale=-1.0).then_inc(s_ze, 1)
                act.wait_ge(s_ze, j + 1)
                act.activation(z_abs, z_abs, ACT.Ln, bias=1.0).then_inc(s_zl, 1)

            def weights(j):
                act.wait_ge(s_zd, j + 1)
                if j >= 1:
                    act.wait_ge(s_zo, j)
                act.activation(z_a, z_ls, ACT.Exp).then_inc(s_za, 1)

            def z_hi(m):
                act.wait_ge(s_zo, 2 * m + 2)
                act.activation(oT_hi[:, 4 * m:4 * m + 4, :].rearrange("p g (h t) -> p h g t", h=NH),
                               ps[:, 6:8, :].rearrange("p h (g t) -> p h g t", g=GRP),
                               ACT.Copy).then_inc(s_zhi, 1)

            softplus_parts(0)
            for j in range(NKV):
                weights(j)
                if j + 1 < NKV:
                    softplus_parts(j + 1)
                if j % 2:
                    z_hi(j // 2)
            for n in range(4):
                hi(C_BO + n + RING)
            squares(9, 8)
            turned(TURN[9], C_F4 - 1)
            feed_forward(4, ffns[4][0])
            squares(10, 9)

        @block.vector
        def _(dve):
            def lo(c, slot=None):
                if isinstance(c, int) and c >= N_CHUNKS:
                    return
                dve.wait_ge(s_hi, c + 1)
                slot = c % RING if slot is None else slot
                dve.tensor_tensor(w_lo[:, slot, :], raw[:, slot, :], f32(w_hi[:, slot, :]),
                                  ALU.subtract).then_inc(s_lo, 1)

            def normalise(n, dst):
                for h in range(NH):
                    i = 2 * n + h
                    dve.wait_ge(s_rstd, i + 1)
                    dve.wait_ge(s_gain[n % 2], 16 * (n // 2 + 1))
                    dve.scalar_tensor_tensor(out=dst[:, h, :], in0=X[:, h, :],
                                             scalar=rstd[:, i:i + 1], in1=gain[:, n % 2, :],
                                             op0=ALU.mult, op1=ALU.mult).then_inc(s_xn, 1)

            def turned(i):
                for h in range(NH):
                    for g in range(2):
                        dve.wait_ge(s_xhi, 4 * i + 2 * h + g + 1)
                        t = (slice(None), slice(4 * g, 4 * g + 4), slice(h * P, (h + 1) * P))
                        dve.tensor_tensor(xT_lo[t], ps[:, 2 * h + g, :].rearrange("p (k n) -> p k n", k=4),
                                          f32(xT_hi[t]), ALU.subtract).then_inc(s_xlo, 1)

            def update(c, scale, base=0):
                for h in range(NH):
                    dve.wait_ge(s_mm, 2 * c + h + 1)
                    dve.scalar_tensor_tensor(out=X[:, h, :], in0=acc(h, base), scalar=scale,
                                             in1=X[:, h, :], op0=ALU.mult,
                                             op1=ALU.add).then_inc(s_xup, 1)

            def feed_forward(f, c0):
                j0 = f * NJ

                def h_lo(j):
                    dve.wait_ge(s_hhi, j + 1)
                    dve.tensor_tensor(oT_lo[:, 0:2, :], ps[:, 6, :].rearrange("p (t s) -> p t s", t=2),
                                      f32(oT_hi[:, 0:2, :]), ALU.subtract).then_inc(s_hlo, 1)

                def gated(j):
                    for h in range(NH):
                        dve.wait_ge(s_silu, j * 2 + (h + 1))
                        dve.tensor_tensor(h_tm[:, h, :], ps[:, 4 + h, GW:2 * GW], silu[:, h, :],
                                          ALU.mult).then_inc(s_h, 1)

                lo(c0 + 3)
                gated(j0)
                lo(c0 + 4)
                h_lo(j0)
                lo(c0 + 5)
                gated(j0 + 1)
                lo(c0 + 6)
                lo(c0 + 7)
                def step(i):
                    h_lo(i + (j0 + 1))
                    lo(i * 3 + (c0 + 5 + RING), (c0 + 5) % RING)
                    gated(i + (j0 + 2))
                    lo(i * 3 + (c0 + 6 + RING), (c0 + 6) % RING)
                    lo(i * 3 + (c0 + 7 + RING), (c0 + 7) % RING)

                last = c0 == C_F4
                with dve.Fori(0, NJ - 2 - last) as i:
                    step(i)
                if last:
                    step(NJ - 3)
                h_lo(j0 + NJ - 1)

            dve.wait_ge(s_parT, 1)
            dve.tensor_copy(par[:, :], ps[:, 7, 0:P]).then_inc(s_parc, 1)
            normalise(0, xn)
            lo(0)
            turned(TURN[0])
            lo(1)
            lo(2)
            dve.wait_ge(s_parc, 1)
            lam = par[:, 56:64]
            neg, e, den, r, r2, t_ = (spt[:, i, :] for i in range(6))
            dve.scalar_tensor_tensor(out=neg, in0=lam, scalar=-1.0, in1=lam, op0=ALU.mult,
                                     op1=ALU.max).then_inc(s_sp, 1)
            dve.wait_ge(s_spe, 1)
            steps = [1]

            def step(ins):
                steps[0] += 1
                ins.then_inc(s_sp, 1)
                dve.wait_ge(s_sp, steps[0])

            step(dve.tensor_scalar(den, e, 2.0, None, ALU.add))
            step(dve.reciprocal(den, den))
            step(dve.tensor_tensor(r, e, den, ALU.mult))
            step(dve.tensor_tensor(r2, r, r, ALU.mult))
            step(dve.tensor_scalar(t_, r2, 1.0 / 17, None, ALU.mult))
            for k in (15, 13, 11, 9, 7, 5, 3):
                step(dve.scalar_tensor_tensor(out=t_, in0=t_, scalar=1.0 / k, in1=r2,
                                              op0=ALU.add, op1=ALU.mult))
            step(dve.scalar_tensor_tensor(out=t_, in0=t_, scalar=1.0, in1=r, op0=ALU.add,
                                          op1=ALU.mult))
            step(dve.tensor_scalar(neg, lam, -1.0, 0.0, ALU.mult, ALU.max))
            step(dve.scalar_tensor_tensor(out=t_, in0=t_, scalar=2.0, in1=neg, op0=ALU.mult,
                                          op1=ALU.add))
            step(dve.tensor_scalar(sp4[:, 0:8], t_, 4.0, None, ALU.mult))
            step(dve.tensor_scalar(sp4[:, 8:16], t_, -4.0, None, ALU.mult))
            step(dve.tensor_scalar(half_b[:, :], par[:, 40:56], 0.5, None, ALU.mult))
            assert steps[0] == SP_DONE


            def band_scores(i):
                dve.wait_ge(s_sc, i + 1)
                dve.wait_ge(s_mask, i + 1)
                dve.scalar_tensor_tensor(out=sbuf_s[:, i % 2, :], in0=ps[:, i % 2, 0:384],
                                         scalar=HD ** -0.5, in1=bias_t[:, i % 3, :],
                                         op0=ALU.mult, op1=ALU.add).then_inc(s_sb, 1)
                dve.wait_ge(s_sb, i + 1)
                for h, (c0, n) in enumerate(((0, P), (P, S))):
                    dve.tensor_reduce(stat[:, i % 2, h:h + 1], sbuf_s[:, i % 2, c0:c0 + n], AX, ALU.max,
                                      negate=True).then_inc(s_max, 1)

            def band_norm(i):
                dve.wait_ge(s_exp, 2 * i + 2)
                dve.reciprocal(stat[:, i % 2, 2:4], stat[:, i % 2, 2:4]).then_inc(s_rec, 1)
                dve.wait_ge(s_rec, i + 1)
                for h, (c0, n) in enumerate(((0, P), (P, S))):
                    dve.tensor_scalar(sbuf_s[:, i % 2, c0:c0 + n], sbuf_s[:, i % 2, c0:c0 + n],
                                      stat[:, i % 2, 2 + h:3 + h], None, ALU.mult).then_inc(s_pn, 1)

            def o_lo(t):
                dve.wait_ge(s_ohi, t + 1)
                dve.tensor_tensor(oT_lo[:, t, :], ps[:, 3, 0:S],
                                  f32(oT_hi[:, t, :]), ALU.subtract).then_inc(s_olo, 1)

            def convolve(t):
                dve.wait_ge(s_slab, SLAB_AT["xr", t // 4])
                dve.tensor_scalar(xc[:, t, :], xrp[:, t, 3:3 + S], par[:, 24 + t:25 + t],
                                  par[:, 32 + t:33 + t], ALU.mult, ALU.add).then_inc(s_cv, 1)
                for n in range(1, 4):
                    dve.wait_ge(s_cv, 4 * t + n)
                    w = 8 * (3 - n) + t
                    dve.scalar_tensor_tensor(out=xc[:, t, :], in0=xrp[:, t, 3 - n:3 - n + S],
                                             scalar=par[:, w:w + 1], in1=xc[:, t, :],
                                             op0=ALU.mult, op1=ALU.add).then_inc(s_cv, 1)

            def gate_products(t):
                dve.wait_ge(s_ra, 4 * t + 4)
                dve.scalar_tensor_tensor(out=xc[:, t, :], in0=rg_t[:, 1, :], scalar=1.0,
                                         in1=xc[:, t, :], op0=ALU.add, op1=ALU.mult).then_inc(s_rd, 1)
                dve.tensor_tensor(rg_t[:, 2, :], xrp[:, t, 3:3 + S], xrp[:, t, 3:3 + S],
                                  ALU.mult).then_inc(s_rd, 1)
                dve.wait_ge(s_rd, 3 * t + 2)
                dve.scalar_tensor_tensor(out=th[:, t, :], in0=rg_t[:, 2, :], scalar=1.0,
                                         in1=th[:, t, :], op0=ALU.add, op1=ALU.mult).then_inc(s_rd, 1)

            for c in range(28):
                i, t = c - HEAD0, c - GATE0
                if 0 <= i < HEADS:
                    band_scores(i)
                if 0 <= i < HEADS:
                    band_norm(i)
                if 0 <= t < KD:
                    gate_products(t)
                if 0 <= t + 1 < KD:
                    convolve(t + 1)
                s, a = c // 2, c % 2
                if a and s >= 10:
                    dve.wait_ge(s_sc, (8, 8, 16, 16)[s - 10])
                    dve.wait_ge(s_bm[s % 2], 16 * ((s - 10) // 2 + 1))
                    for h in range(NH):
                        dve.wait_ge(s_mm, 2 * c + h + 1)
                        dve.tensor_tensor(qk[:, s - 10, h * 512:(h + 1) * 512],
                                          ps[:, slab_banks(s) + h, :],
                                          b_mrg[:, (s % 2) * 512:(s % 2 + 1) * 512],
                                          ALU.add).then_inc(s_bsum, 1)
                lo(c + RING)
                if 1 <= i <= HEADS and (i - 1) % 2:
                    o_lo((i - 1) // 2)

            dve.wait_ge(s_sqrt, 1)
            dve.tensor_tensor(xc[:, :, :], th[:, :, :], xc[:, :, :], ALU.mult).then_inc(s_bx, 1)
            dve.wait_ge(s_bx, 1)
            for t in range(KD):
                dve.tensor_tensor_scan(th[:, t, :], xrp[:, t, 3:3 + S], xc[:, t, :], 0.0,
                                       ALU.mult, ALU.add).then_inc(s_scan, 1)
            lo(C_AO + RING)
            for h in range(2):
                dve.wait_ge(s_scan, 4 * h + 4)
                tiles = slice(4 * h, 4 * h + 4)
                dve.tensor_tensor(xc[:, tiles, :], th[:, tiles, :], gr[:, tiles, :],
                                  ALU.mult).then_inc(s_y, 1)
            for h in range(2):
                tiles = slice(4 * h, 4 * h + 4)
                dve.wait_ge(s_yhi, h + 1)
                dve.tensor_tensor(xT_lo[:, tiles, :], xc[:, tiles, :], f32(xT_hi[:, tiles, :]),
                                  ALU.subtract).then_inc(s_ylo, 1)
            for n in range(1, 4):
                lo(C_AO + n + RING)

            def merge(c, base, gate0, dst, h):
                dve.wait_ge(s_mm, 2 * c + h + 1)
                g = qk[:, gate0:gate0 + 2, h * 512:(h + 1) * 512]
                return dve.scalar_tensor_tensor(
                    out=dst[:, h, :].rearrange("p (a n) -> p a n", a=2), in0=g, scalar=1.0,
                    in1=ps[:, base + 2 * h:base + 2 * h + 2, :], op0=ALU.add, op1=ALU.mult)

            ya = v_tm
            dve.wait_ge(s_slab, 28)
            for h in range(NH):
                merge(C_AO + 3, 0, 0, ya, h).then_inc(s_mrg, 1)
            for n in range(4):
                lo(C_RO + n + RING)
            for h in range(NH):
                merge(C_RO + 3, 4, 2, xn, h).then_inc(s_mrg, 1)
                dve.wait_ge(s_mrg, 3 + h)
                dve.tensor_tensor(xn[:, h, :], xn[:, h, :], ya[:, h, :], ALU.add).then_inc(s_xn, 1)
            turned(TURN["merge"])
            for n in range(4):
                lo(C_WO + n + RING) if n < 3 else None
            update(C_WO + 3, 0.5, 4)
            lo(C_WO + 3 + RING)
            normalise(1, xn)
            turned(TURN[1])
            feed_forward(0, ffns[0][0])
            update(C_F1 - 1, 1.0)
            for h in range(NH):
                dve.wait_ge(s_rstd, 2 * 2 + h + 1)
                dve.wait_ge(s_gain[0], 32)
                dve.scalar_tensor_tensor(out=X[:, h, :], in0=X[:, h, :],
                                         scalar=rstd[:, 4 + h:5 + h], in1=gain[:, 0, :],
                                         op0=ALU.mult, op1=ALU.mult).then_inc(s_xup, 1)
            normalise(3, xn)
            turned(TURN[3])
            lo(C_F1 + 2)
            feed_forward(1, ffns[1][0])

            update(C_AI - 1, 0.5)
            normalise(4, xn)
            turned(TURN[4])
            lo(C_AI + 2)
            for s in range(8):
                for a in range(2):
                    lo(C_AI + 2 * s + a + RING)
                if s < 4:
                    for h in range(NH):
                        dve.wait_ge(s_ge, 2 * s + h + 1)
                        dve.bn_stats(bn[:, h, s, :], g_tm[:, h, 512 * s:512 * (s + 1)]).then_inc(s_bn, 1)
                if s == 3:
                    dve.wait_ge(s_bn, 8)
                    for h in range(NH):
                        dve.bn_aggr(mv[:, h, :], bn[:, h, :, :]).then_inc(s_mv, 1)
                if s in (4, 5):
                    h = s - 4
                    if h == 0:
                        dve.wait_ge(s_ln, 32)
                    dve.wait_ge(s_lrs, h + 1)
                    dve.tensor_scalar(g_tm[:, h, :], g_tm[:, h, :], mv[:, h, 0:1], ln_rs[:, h, 1:2],
                                      ALU.subtract, ALU.mult).then_inc(s_lv, 1)
                    dve.wait_ge(s_lv, 3 * h + 1)
                    dve.tensor_tensor(g_tm[:, h, :], g_tm[:, h, :], ln_g, ALU.mult).then_inc(s_lv, 1)
                    dve.wait_ge(s_lv, 3 * h + 2)
                    dve.tensor_tensor(g_tm[:, h, :], g_tm[:, h, :], ln_b, ALU.add).then_inc(s_lv, 1)

            def gated(g):
                dve.wait_ge(s_spa, g + 1)
                if g >= 2:
                    dve.wait_ge(s_uvT, g - 1)
                for h in range(NH):
                    dve.scalar_tensor_tensor(out=uv[:, g % 2, h, :],
                                             in0=ps[:, 4 + g % 2, h * GW:(h + 1) * GW],
                                             scalar=par[:, 64 + g:65 + g],
                                             in1=u_tm[:, h, g * GW:(g + 1) * GW],
                                             op0=ALU.add, op1=ALU.mult).then_inc(s_uv, 1)

            def uv_lo(g):
                dve.wait_ge(s_uhi, g + 1)
                t = (slice(None), slice(2 * (g % 2), 2 * (g % 2) + 2), slice(None))
                dve.tensor_tensor(oT_lo[t], ps[:, 6 + g % 2, :].rearrange("p (t s) -> p t s", t=2),
                                  f32(oT_hi[t]), ALU.subtract).then_inc(s_ulo, 1)

            gated(0)
            gated(1)
            uv_lo(0)
            for g in range(NG):
                if g + 2 < NG:
                    gated(g + 2)
                if g + 1 < NG:
                    uv_lo(g + 1)
                lo(C_AW + g + RING) if g < NG - 1 else None
            update(C_F2 - 1, 1.0)
            lo(C_F2 - 1 + RING)
            normalise(5, xn)
            turned(TURN[5])
            feed_forward(2, ffns[2][0])

            update(C_KV - 1, 0.5)
            normalise(6, xn)
            turned(TURN[6])
            for n in range(3):
                lo(C_KV + 2 + n)
            normalise(7, xn)
            turned(TURN[7])
            feed_forward(3, ffns[3][0])

            update(C_Q - 1, 0.5)
            normalise(8, xn)
            turned(TURN[8])
            for n in range(5):
                lo(C_Q + 2 + n)

            diag = before[:, :].rearrange("p (o t) -> p o t", o=1).broadcast_to([P, GRP, P])

            def softplus(j):
                dve.wait_ge(s_zl, j + 1)
                if j >= 1:
                    dve.wait_ge(s_ex, j)
                    dve.wait_ge(s_za, j)
                dve.scalar_tensor_tensor(out=z_sp, in0=ps[:, 0:3, :], scalar=0.0, in1=z_abs,
                                         op0=ALU.max, op1=ALU.add).then_inc(s_zs, 1)
                dve.scalar_tensor_tensor(out=z_ls, in0=ps[:, 0:3, :], scalar=0.0, in1=z_abs,
                                         op0=ALU.min, op1=ALU.subtract).then_inc(s_zs, 1)
                dve.wait_ge(s_zs, 2 * j + 1)
                for b in (0, 2):
                    blk = z_sp[:, b, :].rearrange("p (g t) -> p g t", g=GRP)
                    dve.tensor_tensor(blk, blk, diag, ALU.mult).then_inc(s_zm, 1)

            def exponent(j):
                dve.wait_ge(s_ex, j + 1)
                dve.wait_ge(s_zs, 2 * j + 2)
                dve.tensor_tensor(z_ls, z_ls, ps[:, 3:6, :], ALU.subtract).then_inc(s_zd, 1)

            def masked(j):
                dve.wait_ge(s_za, j + 1)
                for b in (0, 2):
                    blk = z_a[:, b, :].rearrange("p (g t) -> p g t", g=GRP)
                    dve.tensor_tensor(blk, blk, diag, ALU.mult).then_inc(s_zam, 1)

            def z_lo(m):
                dve.wait_ge(s_zhi, m + 1)
                for h in range(NH):
                    t = (slice(None), slice(4 * m, 4 * m + 4), slice(h * P, (h + 1) * P))
                    ins = dve.tensor_tensor(oT_lo[t], ps[:, 6 + h, :].rearrange("p (g t) -> p g t", g=GRP),
                                            f32(oT_hi[t]), ALU.subtract)
                ins.then_inc(s_zlo, 1)

            softplus(0)
            for j in range(NKV):
                exponent(j)
                masked(j)
                if j + 1 < NKV:
                    softplus(j + 1)
                if j % 2:
                    z_lo(j // 2)
            for n in range(3):
                lo(C_BO + n + RING)
            update(C_F4 - 1, 1.0)
            lo(C_F4 - 1 + RING)
            normalise(9, xn)
            turned(TURN[9])
            feed_forward(4, ffns[4][0])
            update(N_CHUNKS - 1, 0.5)
            normalise(10, xn)
    return nc


SP_DONE = 19
SLAB_AT = {s: 2 * (n + 1) for n, s in enumerate(SLABS)}
XN_AT = {0: 0, 1: 4, 2: 4, 3: 6, 4: 8, 5: 10, 6: 12, 7: 14, 8: 16, 9: 18, 10: 20}
XUP = {v: 2 * (v - 1) for v in range(1, 10)}

_INS = ["x", "norm_mix_g", "w_in", "b_merge", "rel_rev", "w_attn_out", "conv_w", "conv_b", "w_rg_r",
        "b_rg_r", "w_rg_i", "b_rg_i", "rg_lambda", "w_rnn_out", "w_o", "norm_ffn_g", "w_ffn_in",
        "w_ffn_out", "final_norm_g", "ffn_norm_2", "ffn_w_in_2", "ffn_w_out_2", "mix_norm_2",
        "a_w_in_2", "a_ln_g_2", "a_ln_b_2", "a_w_s_2", "a_b_s_2", "a_w_out_2", "kv_norm_2",
        "w_kv_2", "b_w_q_2", "b_w_o_2", "final_norm_2"]
_ONE_LAYER = ("norm_mix_g", "w_in", "b_merge", "rel_table", "w_attn_out", "conv_w", "conv_b",
              "w_rg_r", "b_rg_r", "w_rg_i", "b_rg_i", "rg_lambda", "w_rnn_out", "w_o", "norm_ffn_g",
              "w_ffn_in", "w_ffn_out", "a_w_in_2", "a_ln_g_2", "a_ln_b_2", "a_w_s_2", "a_b_s_2",
              "a_w_out_2", "b_w_q_2", "b_w_o_2", "x")


def kernel(**inputs):
    import numpy as _np
    import concourse.bacc as _bacc
    from concourse import mybir as _mybir
    from concourse.bass_utils import run_bass_kernel_spmd as _run

    arrays = {k: _np.asarray(v) for k, v in inputs.items()}
    for name in _ONE_LAYER:
        arrays[name] = arrays[name][0]
    table = arrays.pop("rel_table")
    arrays["rel_rev"] = _np.pad(table[:, 1:][:, ::-1], ((0, 0), (127, 1)), mode="edge")

    arrays["b_w_q_2"] = arrays["b_w_q_2"].reshape(D, 2, 2, GRP, HD).transpose(0, 1, 3, 2, 4).reshape(D, D)

    nc = _bacc.Bacc("TRN2", target_bir_lowering=False, num_devices=1)
    feed, d = {}, {}
    for name in _INS:
        a = _np.ascontiguousarray(arrays[name])
        feed[f"in_{name}"] = a
        d[name] = nc.dram_tensor(f"in_{name}", a.shape, _mybir.dt.from_np(a.dtype),
                                 kind="ExternalInput").ap()
    out = nc.dram_tensor("out_0", (S, D), F32, kind="ExternalOutput").ap()
    build(nc, d, out)
    r = _run(nc, [feed], core_ids=[0])
    return r.results[0]["out_0"].reshape(1, S, D)
```

```python
from contextlib import ExitStack

import concourse.bass as bass
from concourse import mybir

F32 = mybir.dt.float32
F32R = mybir.dt.float32r
ALU = mybir.AluOpType
ACT = mybir.ActivationFunctionType
AX = mybir.AxisListType.X

P = 128
D = 1024
S = 256
NH = S // P
KD = D // P
DFF = 2816
GW = 256
NJ = DFF // GW
HEADS = 16
HD = 64
EPS = 1e-6
LN_EPS = 1e-5
NEG = -1e30
TAB = 384
DA = 2 * D
NG = 8
NKV = 4
GRP = HEADS // NKV

RING = 3
CH = 2048

C_IN = 0
C_AO = C_IN + 28
C_RO = C_AO + 4
C_WO = C_RO + 4
C_F0 = C_WO + 4
C_F1 = C_F0 + 3 * NJ
C_AI = C_F1 + 3 * NJ
C_AW = C_AI + 16
C_F2 = C_AW + 8
C_F3 = C_F2 + 3 * NJ
C_KV = C_F3 + 2
C_Q = C_F3 + 3 * NJ + 2
C_BO = C_Q + 4
C_F4 = C_BO + 4
N_CHUNKS = C_F4 + 3 * NJ

SLABS = [("v", 0), ("xr", 0), ("xr", 1), ("q", 0), ("k", 0), ("q", 1), ("k", 1), ("v", 1),
         ("gr", 0), ("gr", 1), ("ga", 0), ("ga", 1), ("gb", 0), ("gb", 1)]
COL0 = {"q": 0, "k": D, "v": 2 * D, "xr": 3 * D, "gr": 4 * D, "ga": 5 * D, "gb": 6 * D}
FM_SLABS = ("q", "k", "xr", "gr")
HEAD0 = 11
GATE0 = 5

N_IN, N_F0, N_END1, N_F1, N_AI, N_F2, N_F3, N_Q, N_F4, N_END2 = range(10)
N_NORMS = 10
U_MERGE, U_WO, U_F0, U_F1, U_AW, U_F2, U_F3, U_BO, U_F4 = range(-1, 8)
T_IN, T_MERGE, T_F0, T_F1, T_AI, T_F2, T_F3, T_Q, T_F4 = range(9)
G_IN, G_F0, G_F1, G_AI, G_F2, G_KV, G_F3, G_Q, G_F4, G_END1 = range(P, P + 80, 8)


def build(nc, d, out):
    ctx = ExitStack()
    with ctx:
        def sb(name, shape, dt=F32):
            return ctx.enter_context(nc.sbuf_tensor(name, shape, dt))

        def sem(name):
            return ctx.enter_context(nc.semaphore(name))

        ps = ctx.enter_context(nc.psum_tensor("ps", [P, 8, 512], F32))

        raw = sb("raw", [P, RING, CH])
        w_hi = sb("w_hi", [P, RING, CH], F32R)
        w_lo = sb("w_lo", [P, RING, CH], F32R)
        X = sb("X", [P, NH, D])
        xn = sb("xn", [P, NH, D])
        xT_hi = sb("xT_hi", [P, KD, S], F32R)
        xT_lo = sb("xT_lo", [P, KD, S], F32R)
        oT_hi = sb("oT_hi", [P, KD, S], F32R)
        oT_lo = sb("oT_lo", [P, KD, S], F32R)
        ident = sb("ident", [P, P])
        ones = sb("ones", [P, P])
        later = sb("later", [P, P])
        before = sb("before", [P, P])
        rows = sb("rows", [P, 2, P])
        cols = sb("cols", [P, 2 * P])
        par = cols[:, 0:P]
        g_f1 = sb("g_f1", [P, KD])
        diag_r = sb("diag_r", [P, S])
        R = sb("R", [P, S])
        half_b = sb("half_b", [P, 16])
        sp4 = sb("sp4", [P, 16])
        spt = sb("spt", [P, 6, 8])
        ss = sb("ss", [P, 2 * N_NORMS])
        var = sb("var", [P, 2 * N_NORMS])
        rstd = sb("rstd", [P, 2 * N_NORMS])
        nf = sb("nf", [P, 4])
        minus_half = sb("minus_half", [P, 1])
        row_b = sb("row_b", [P, D])
        mem = sb("mem", [P, 18200])

        def view(at, *dims):
            n = 1
            for x in dims:
                n *= x
            v = mem[:, at:at + n]
            names = "abcd"[:len(dims)]
            if len(dims) == 1:
                return v
            return v.rearrange("p (" + " ".join(names) + ") -> p " + " ".join(names),
                               **{names[i]: dims[i] for i in range(1, len(dims))})

        qk = view(0, 4, 1024)
        v_tm = view(4096, NH, D)
        gr = view(6144, KD, S)
        xrp = view(8192, KD, S + 3)
        xc = view(10272, KD, S)
        bias_t = view(12320, 3, 384)
        sbuf_s = view(13472, 2, 384)
        pT = view(14240, 2, 384)
        rg_t = view(15008, 3, S)
        w_bd = view(15776, 2, KD, P)
        th = xn[:, :, :].rearrange("p h d -> p (h d)").rearrange("p (t s) -> p t s", s=S)
        stat = sb("stat", [P, 2, 4])
        silu = view(0, NH, GW)
        h_tm = view(512, NH, GW)
        u_tm = view(0, NH, DA)
        g_tm = view(4096, NH, DA)
        ln_g = view(8192, DA)
        ln_b = view(10240, DA)
        ws_t = view(12288, NG, P)
        ws_r = view(13312, NG, P)
        uv = view(14336, 2, NH, GW)
        bn = sb("bn", [P, NH, 4, 6])
        mv = sb("mv", [P, NH, 2])
        ln_rs = sb("ln_rs", [P, NH, 2])
        q_b = view(0, KD, S)
        k_b = view(16384, 2, S)
        v_b = view(16384 + 512, NH, 256)
        z_abs = view(2048, 2, 3, 512)
        z_sp = view(5120, 2, 3, 512)
        z_ls = view(8192, 2, 3, 512)
        z_a = view(11264, 2, 3, 512)

        skew = nc.dram_tensor("skew", (HEADS, P * TAB), F32, kind="Internal").ap()

        s_skew = [sem(f"s_skew{i}") for i in range(3)]
        s_x = [sem("s_x0"), sem("s_x1")]
        s_hi0 = sem("s_hi0")
        s_lo0 = sem("s_lo0")
        s_g1 = sem("s_g1")
        s_g2 = sem("s_g2")
        s_raw = [sem(f"s_raw{i}") for i in range(RING)]
        s_hi = sem("s_hi")
        s_lo = sem("s_lo")
        s_mm = sem("s_mm")
        s_const = sem("s_const")
        s_par = sem("s_par")
        s_parT = sem("s_parT")
        s_parc = sem("s_parc")
        s_sp = sem("s_sp")
        s_spe = sem("s_spe")
        s_xup = sem("s_xup")
        s_half = sem("s_half")
        s_sq = sem("s_sq")
        s_var = sem("s_var")
        s_rstd = sem("s_rstd")
        s_nf = sem("s_nf")
        s_xn = sem("s_xn")
        s_xg = sem("s_xg")
        s_gf = sem("s_gf")
        s_diag = sem("s_diag")
        s_R = sem("s_R")
        s_Rc = sem("s_Rc")
        s_turn = sem("s_turn")
        s_xhi = sem("s_xhi")
        s_xlo = sem("s_xlo")
        s_out = sem("s_out")
        s_slab = sem("s_slab")
        s_bsum = sem("s_bsum")
        s_bm = [sem("s_bm0"), sem("s_bm1")]
        s_bias = [sem(f"s_bias{i}") for i in range(3)]
        s_mask = sem("s_mask")
        s_sc = sem("s_sc")
        s_sb = sem("s_sb")
        s_max = sem("s_max")
        s_exp = sem("s_exp")
        s_rec = sem("s_rec")
        s_pn = sem("s_pn")
        s_pt = sem("s_pt")
        s_ptc = sem("s_ptc")
        s_pv = sem("s_pv")
        s_ohi = sem("s_ohi")
        s_olo = sem("s_olo")
        s_wbd = sem("s_wbd")
        s_z0 = sem("s_z0")
        s_cv = sem("s_cv")
        s_gt = sem("s_gt")
        s_ra = sem("s_ra")
        s_rd = sem("s_rd")
        s_sqrt = sem("s_sqrt")
        s_bx = sem("s_bx")
        s_scan = sem("s_scan")
        s_y = sem("s_y")
        s_yhi = sem("s_yhi")
        s_ylo = sem("s_ylo")
        s_mrg = sem("s_mrg")
        s_silu = sem("s_silu")
        s_h = sem("s_h")
        s_hT = sem("s_hT")
        s_hhi = sem("s_hhi")
        s_hlo = sem("s_hlo")
        s_ln = sem("s_ln")
        s_ws = sem("s_ws")
        s_wsm = sem("s_wsm")
        s_wsT = sem("s_wsT")
        s_wsc = sem("s_wsc")
        s_ge = sem("s_ge")
        s_bn = sem("s_bn")
        s_mv = sem("s_mv")
        s_lve = sem("s_lve")
        s_lrs = sem("s_lrs")
        s_lv = sem("s_lv")
        s_spa = sem("s_spa")
        s_uv = sem("s_uv")
        s_uvT = sem("s_uvT")
        s_uhi = sem("s_uhi")
        s_ulo = sem("s_ulo")
        s_k = sem("s_k")
        s_v = sem("s_v")
        s_q = sem("s_q")
        s_z = sem("s_z")
        s_ab = sem("s_ab")
        s_ze = sem("s_ze")
        s_zl = sem("s_zl")
        s_zsp = sem("s_zsp")
        s_zls = sem("s_zls")
        s_zm = sem("s_zm")
        s_ex = sem("s_ex")
        s_zd = sem("s_zd")
        s_za = sem("s_za")
        s_zam = sem("s_zam")
        s_zo = sem("s_zo")
        s_zhi = sem("s_zhi")
        s_zlo = sem("s_zlo")

        def acc(h, base=0):
            return ps[:, base + 2 * h:base + 2 * h + 2, :].rearrange("p b n -> p (b n)")

        def slab_banks(s):
            return 4 + 2 * (s % 2)

        def f32(ap):
            return ap.bitcast(F32)

        def gain(g, k):
            return g_f1[:, k:k + 1] if g == G_F1 else cols[:, g + k:g + k + 1]

        def chunk_gain(c):
            for c0, n, g in ((C_IN, 28, G_IN), (C_AI, 16, G_AI), (C_KV, 2, G_KV), (C_Q, 4, G_Q)):
                if c0 <= c < c0 + n:
                    return g, 4 * ((c - c0) % 2)
            for c0, g in ((C_F0, G_F0), (C_F1, G_F1), (C_F2, G_F2), (C_F3, G_F3), (C_F4, G_F4)):
                if c in (c0, c0 + 1):
                    return g, 4 * (c - c0)
                c0 += 2 if c0 == C_F3 else 0
                if c in (c0 + 2, c0 + 3):
                    return g, 4 * (c - c0 - 2)
                if c0 + 5 <= c < c0 + 3 * NJ - 1 and (c - c0 - 5) % 3 < 2:
                    return g, 4 * ((c - c0 - 5) % 3)
            return None

        block = ctx.enter_context(nc.Block())

        @block.sync
        def _(sp):
            def load(c, slot):
                sp.dma_start(raw[:, slot, :], d["stream"][c, :, :]).then_inc(s_raw[slot], 16)

            for h in range(NH):
                sp.dma_start(X[:, h, :], d["x"][h * P:(h + 1) * P, :]).then_inc(s_x[h], 16)
                if h == 0:
                    sp.dma_start(rows[:, :, :], d["params"].rearrange("(a r) n -> r a n", a=2)
                                 ).then_inc(s_par, 16)
            for c in range(RING):
                load(c, c)
            with sp.Fori(0, N_CHUNKS // RING - 1) as i:
                for slot in range(RING):
                    sp.wait_ge(s_lo, i * RING + (slot + 1))
                    sp.dma_start(raw[:, slot, :], d["stream"][bass.ds(i * RING + (RING + slot), 1), :, :]
                                 .rearrange("o p n -> p (o n)")).then_inc(s_raw[slot], 16)
            for c in range(N_CHUNKS // RING * RING, N_CHUNKS):
                sp.wait_ge(s_lo, c - RING + 1)
                load(c, c % RING)
            for h in range(NH):
                sp.wait_ge(s_xn, XN_END + h + 1)
                sp.dma_start(out[h * P:(h + 1) * P, :], xn[:, h, :]).then_inc(s_out, 16)
            sp.wait_ge(s_out, 32)

        @block.gpsimd
        def _(pool):
            def norm(n):
                for h in range(NH):
                    i = 2 * n + h
                    pool.wait_ge(s_sq, i + 1)
                    pool.tensor_scalar(var[:, i:i + 1], ss[:, i:i + 1], 1.0 / D, EPS,
                                       ALU.mult, ALU.add).then_inc(s_var, 1)
                    pool.wait_ge(s_var, i + 1)
                    pool.tensor_tensor(rstd[:, i:i + 1], var[:, i:i + 1], minus_half[:, :],
                                       ALU.pow).then_inc(s_rstd, 1)

            def norm_f1():
                for h in range(NH):
                    i, j = 2 * N_F1 + h, 2 * N_END1 + h
                    a, b = nf[:, 2 * h:2 * h + 1], nf[:, 2 * h + 1:2 * h + 2]
                    r = rstd[:, j:j + 1]
                    pool.wait_ge(s_rstd, j + 1)
                    pool.tensor_tensor(a, r, r, ALU.mult).then_inc(s_nf, 1)
                    pool.wait_ge(s_nf, 3 * h + 1)
                    pool.wait_ge(s_sq, i + 1)
                    pool.tensor_tensor(b, a, ss[:, i:i + 1], ALU.mult).then_inc(s_nf, 1)
                    pool.wait_ge(s_nf, 3 * h + 2)
                    pool.tensor_scalar(var[:, i:i + 1], b, 1.0 / D, EPS,
                                       ALU.mult, ALU.add).then_inc(s_var, 1)
                    pool.wait_ge(s_var, i + 1)
                    pool.tensor_tensor(a, var[:, i:i + 1], minus_half[:, :],
                                       ALU.pow).then_inc(s_nf, 1)
                    pool.wait_ge(s_nf, 3 * h + 3)
                    pool.tensor_tensor(rstd[:, i:i + 1], a, r, ALU.mult).then_inc(s_rstd, 1)

            def all_rows(dst, src):
                n = dst.shape[1]
                return pool.dma_start(dst, src.rearrange("(o n) -> o n", o=1).broadcast_to([P, n]))

            pool.memset(minus_half[:, :], -0.5).then_inc(s_const, 1)
            pool.memset(ident[:, :], 0.0).then_inc(s_const, 1)
            pool.wait_ge(s_const, 2)
            pool.affine_select(out=ident[:, :], in_=ident[:, :], compare_op=ALU.not_equal, fill=1.0,
                               base=0, pattern=[[-1, P]], channel_multiplier=1).then_inc(s_const, 1)
            pool.memset(ones[:, :], 1.0).then_inc(s_const, 1)
            norm(N_IN)
            pool.wait_ge(s_const, 4)
            pool.affine_select(out=later[:, :], in_=ones[:, :], compare_op=ALU.is_gt, fill=0.0,
                               base=0, pattern=[[-1, P]], channel_multiplier=1).then_inc(s_const, 1)
            pool.affine_select(out=before[:, :], in_=ones[:, :], compare_op=ALU.is_gt, fill=0.0,
                               base=0, pattern=[[1, P]], channel_multiplier=-1).then_inc(s_const, 1)
            pool.memset(mem[:, 15776:15776 + 2048], 0.0).then_inc(s_z0, 1)
            pool.memset(xrp[:, :, 0:3], 0.0).then_inc(s_z0, 1)
            pool.wait_ge(s_z0, 2)
            for g, name in enumerate(("w_rg_r", "w_rg_i")):
                src = d[name].rearrange("(t b) i o -> b i t o", b=2)
                for b in range(2):
                    pool.dma_start(w_bd[b * HD:(b + 1) * HD, g, :, b * HD:(b + 1) * HD],
                                   src[b]).then_inc(s_wbd, 16)
            def merge_bias(s):
                all_rows(row_b[:, (s % 2) * 512:(s % 2 + 1) * 512],
                         d["b_merge"][(s - 10) * 512:(s - 9) * 512]).then_inc(s_bm[s % 2], 16)

            merge_bias(10)
            merge_bias(11)

            def copies(i):
                pool.dma_start(skew[i].rearrange("(q n) -> q n", n=TAB),
                               d["rel_rev"][i:i + 1, :].broadcast_to([P, TAB])
                               ).then_inc(s_skew[i % 3], 16)

            for i in range(3):
                copies(i)
            for i in range(HEADS):
                if i >= 3:
                    pool.wait_ge(s_sb, i - 2)
                slot = bias_t[:, i % 3, :]
                pool.wait_ge(s_skew[i % 3], 16 * (i // 3 + 1))
                for off, c0, n in ((128, 0, 128), (0, 128, 256)):
                    src = skew[i, 0:P * (TAB - 1)].rearrange(
                        "(q n) -> q n", n=TAB - 1)[:, P - 1 + off:P - 1 + off + n]
                    pool.dma_start(slot[:, c0:c0 + n], src).then_inc(s_bias[i % 3], 16)
                pool.wait_ge(s_bias[i % 3], 32 * (i // 3 + 1))
                pool.memset(bias_t[0:64, i % 3, 64:128], NEG)
                pool.memset(bias_t[0:64, i % 3, 320:384], NEG).then_inc(s_mask, 1)
                if i + 3 < HEADS:
                    copies(i + 3)
            for s in (12, 13):
                pool.wait_ge(s_bsum, 2 * (s - 11))
                merge_bias(s)
            pool.wait_ge(s_bsum, 8)
            all_rows(row_b[:, :], d["final_norm_g"]).then_inc(s_g1, 16)
            norm(N_F0)
            pool.wait_ge(s_xup, 4 * U_WO + 4)
            all_rows(ln_g, d["a_ln_g_2"]).then_inc(s_ln, 16)
            all_rows(ln_b, d["a_ln_b_2"]).then_inc(s_ln, 16)
            pool.dma_start(ws_r, d["a_w_s_2"].rearrange("g t s -> t g s")).then_inc(s_ws, 16)
            pool.wait_ge(s_ws, 16)
            pool.affine_select(out=ws_r, in_=ws_r, compare_op=ALU.is_ge, fill=0.0, base=0,
                               pattern=[[0, NG], [-1, P]], channel_multiplier=1).then_inc(s_wsm, 1)
            norm(N_END1)
            norm_f1()
            pool.wait_ge(s_xg, 2)
            all_rows(row_b[:, :], d["final_norm_2"]).then_inc(s_g2, 16)
            norm(N_AI)
            for h in range(NH):
                pool.wait_ge(s_mv, h + 1)
                pool.tensor_scalar(ln_rs[:, h, 0:1], mv[:, h, 1:2], 1.0, LN_EPS,
                                   ALU.mult, ALU.add).then_inc(s_lve, 1)
                pool.wait_ge(s_lve, h + 1)
                pool.tensor_tensor(ln_rs[:, h, 1:2], ln_rs[:, h, 0:1], minus_half[:, :],
                                   ALU.pow).then_inc(s_lrs, 1)
            for n in (N_F2, N_F3, N_Q):
                norm(n)
            diag = before[:, :].rearrange("p (o t) -> p o t", o=1).broadcast_to([P, GRP, P])

            def mask_softplus(j):
                for b in (0, 2):
                    pool.wait_ge(s_zsp, 3 * j + b + 1)
                    blk = z_sp[:, j % 2, b, :].rearrange("p (g t) -> p g t", g=GRP)
                    pool.tensor_tensor(blk, blk, diag, ALU.mult).then_inc(s_zm, 1)

            def mask_weights(j):
                pool.wait_ge(s_za, j + 1)
                for b in (0, 2):
                    blk = z_a[:, j % 2, b, :].rearrange("p (g t) -> p g t", g=GRP)
                    pool.tensor_tensor(blk, blk, diag, ALU.mult).then_inc(s_zam, 1)

            pool.wait_ge(s_const, 6)
            mask_softplus(0)
            mask_softplus(1)
            for j in range(2, NKV):
                mask_weights(j - 2)
                mask_softplus(j)
            mask_weights(NKV - 2)
            mask_weights(NKV - 1)
            for n in (N_F4, N_END2):
                norm(n)

        @block.tensor
        def _(pe):
            def product(dst, x, w, start, stop):
                pe.matmul(dst, x[0], w[0], start=start, stop=False, skip_group_check=True)
                pe.matmul(dst, x[0], w[1], start=False, stop=False, skip_group_check=True)
                return pe.matmul(dst, x[1], w[0], start=False, stop=stop, skip_group_check=True)

            def both(t, *index):
                return [x[index] for x in t]

            ALL = slice(None)
            XT = (xT_hi, xT_lo)
            OT = (oT_hi, oT_lo)

            def slot(c0, k):
                return [w[:, c0 % RING, :].rearrange("p (k n) -> p k n", k=k) for w in (w_hi, w_lo)]

            def split(c):
                pe.wait_ge(s_lo, c + 1)

            def tm_cols_half(c0, a, banks, h, turn=None, mid=None):
                w = slot(c0, 4)
                if turn is not None:
                    pe.wait_ge(s_xlo, 4 * turn + 2 * h + a + 1)
                for k in range(4):
                    if k == 2 and mid is not None:
                        mid()
                    m = product(ps[:, banks + h, :],
                                both(XT, ALL, 4 * a + k, slice(h * P, (h + 1) * P)),
                                both(w, ALL, k, ALL), a == 0 and k == 0, a == 1 and k == 3)
                m.then_inc(s_mm, 1)

            def tm_cols(c0, a, banks):
                for h in range(NH):
                    tm_cols_half(c0, a, banks, h)

            def fm_cols(c0, a, banks, turn=None, mid=None):
                w = slot(c0, 4)
                if turn is not None:
                    pe.wait_ge(s_xlo, 4 * turn + 2 + a + 1)
                for t in range(4):
                    if t == 2 and mid is not None:
                        mid()
                    for k in range(4):
                        cols_ = both(w, ALL, k, slice(t * P, (t + 1) * P))
                        x = both(XT, ALL, 4 * a + k, ALL)
                        dst = ps[:, banks + t // 2, (t % 2) * S:(t % 2 + 1) * S]
                        m = product(dst, cols_, x, a == 0 and k == 0 and t % 2 == 0,
                                    a == 1 and k == 3)
                    if t % 2:
                        m.then_inc(s_mm, 1)

            def tm_rows_half(c0, src, k0, base, start, stop, h, mid=None):
                w = slot(c0, 2)
                for n in range(2):
                    if n == 1 and stop:
                        m.then_inc(s_half, 1)
                    if n == 1 and mid is not None:
                        mid()
                    for k in range(2):
                        m = product(ps[:, base + 2 * h + n, :],
                                    both(src, ALL, k0 + k, slice(h * P, (h + 1) * P)),
                                    both(w, ALL, k, slice(n * 512, (n + 1) * 512)),
                                    start and k == 0, stop and k == 1)
                m.then_inc(s_mm, 1)

            def tm_rows(c0, src, k0, base, start, stop):
                for h in range(NH):
                    tm_rows_half(c0, src, k0, base, start, stop, h)

            def turn_tile(src, h, base, signal, before):
                for k in range(KD):
                    if k % 4 == 0:
                        pe.wait_ge(signal, before + k // 4 + 1)
                    m = pe.transpose(acc(h, base)[:, k * P:(k + 1) * P],
                                     src[:, h, k * P:(k + 1) * P], ident[:, :])
                    if k % 4 == 3:
                        m.then_inc(s_turn, 1)

            def turn_x(u, h):
                turn_tile(X, h, 0, s_xup, 4 * u + 2 * h)

            def last_rows(c, src, k0, u, base=0, turn=None):
                turn = turn or (lambda h: turn_x(u, h))
                tm_rows_half(c, src, k0, base, False, True, 0)
                tm_rows_half(c, src, k0, base, False, True, 1, lambda: turn(0))

            def turn_h(j):
                pe.wait_ge(s_h, j * 2 + 2)
                for h in range(NH):
                    for t in range(2):
                        m = pe.transpose(ps[:, 6, t * S + h * P:t * S + (h + 1) * P],
                                         h_tm[:, h, t * P:(t + 1) * P], ident[:, :])
                m.then_inc(s_hT, 1)

            def feed_forward(f, c0, u, turn, after, after_first=None):
                j0 = f * NJ

                def up(c, slot_of, a):
                    split(c)
                    tm_cols(slot_of, a, 4)

                def up_after_kv(c):
                    split(c)
                    tm_cols_half(c, 0, 4, 0)
                    pe.wait_ge(s_v, 2)
                    tm_cols_half(c, 0, 4, 1)

                def features(j):
                    pe.wait_ge(s_hlo, j + 1)

                split(c0)
                tm_cols_half(c0, 0, 6, 0, turn, lambda: turn_x(u, 1))
                tm_cols_half(c0, 0, 6, 1, turn)
                split(c0 + 1)
                for h in range(NH):
                    tm_cols_half(c0 + 1, 1, 6, h, turn)
                if after_first is not None:
                    after_first()
                    c0 += 2
                    up_after_kv(c0 + 2)
                else:
                    up(c0 + 2, c0 + 2, 0)
                turn_h(j0)
                up(c0 + 3, c0 + 3, 1)
                split(c0 + 4)
                features(j0)
                tm_rows(c0 + 4, OT, 0, 0, True, False)
                with pe.Fori(0, NJ - 3) as i:
                    pe.wait_ge(s_h, i * 2 + (2 * j0 + 4))
                    up(i * 3 + (c0 + 5), c0 + 5, 0)
                    turn_h(i + (j0 + 1))
                    up(i * 3 + (c0 + 6), c0 + 6, 1)
                    split(i * 3 + (c0 + 7))
                    features(i + (j0 + 1))
                    tm_rows(c0 + 7, OT, 0, 0, False, False)
                e = c0 + 3 * NJ - 1
                j = j0 + NJ - 1
                pe.wait_ge(s_h, 2 * j)
                up(e - 3, e - 3, 0)
                turn_h(j - 1)
                up(e - 2, e - 2, 1)
                split(e - 1)
                features(j - 1)
                tm_rows_half(e - 1, OT, 0, 0, False, False, 0)
                turn_h(j)
                tm_rows_half(e - 1, OT, 0, 0, False, False, 1)
                split(e)
                features(j)
                if after == U_F4:
                    tm_rows(e, OT, 2, 0, False, True)
                else:
                    last_rows(e, OT, 2, after)

            pe.wait_ge(s_const, 3)
            pe.wait_ge(s_par, 16)
            for n in range(2):
                m = pe.transpose(ps[:, 7, n * P:(n + 1) * P], rows[:, n, :], ident[:, :])
            m.then_inc(s_parT, 1)

            def turn_first(h):
                turn_tile(xn, h, 0, s_xn, 2 * h)

            turn_first(0)
            turn_first(1)

            def scores(i):
                q = qk[:, 2 * (i // 8), :].rearrange("p (t s) -> p t s", s=S)
                k = qk[:, 2 * (i // 8) + 1, :].rearrange("p (t s) -> p t s", s=S)
                rows = slice(HD * (i % 2), HD * (i % 2) + HD)
                t = (i % 8) // 2
                pe.wait_ge(s_slab, SLAB_AT["k", i // 8])
                if i >= 2:
                    pe.wait_ge(s_ptc, i - 1)
                pe.matmul(ps[:, i % 2, 0:P], q[rows, t, 0:P], k[rows, t, 0:P], start=True, stop=True)
                pe.matmul(ps[:, i % 2, P:P + S], q[rows, t, P:S], k[rows, t, :],
                          start=True, stop=True).then_inc(s_sc, 1)

            def turn_p(i):
                pe.wait_ge(s_pn, 2 * i + 2)
                for n in range(3):
                    m = pe.transpose(ps[:, i % 2, n * P:(n + 1) * P],
                                     sbuf_s[:, i % 2, n * P:(n + 1) * P], ident[:, :])
                m.then_inc(s_pt, 1)

            def pv(i):
                pe.wait_ge(s_ptc, i + 1)
                pe.wait_ge(s_slab, SLAB_AT["v", i // 8])
                t = i // 2
                if i % 2 == 0 and t >= 1:
                    pe.wait_ge(s_olo, t)
                o = ps[HD * (i % 2):HD * (i % 2) + HD, 3, 0:S]
                val = [v_tm[:, h, i * HD:(i + 1) * HD] for h in range(NH)]
                pe.matmul(o[:, 0:P], val[0], pT[:, i % 2, 0:P], start=True, stop=True)
                pe.matmul(o[:, P:S], val[0], pT[:, i % 2, P:S], start=True, stop=False)
                pe.matmul(o[:, P:S], val[1], pT[:, i % 2, S:S + P], start=False,
                          stop=True).then_inc(s_pv, 1)

            def gates(t):
                if t == 0:
                    pe.wait_ge(s_wbd, 64)
                pe.wait_ge(s_cv, 4 * t + 4)
                if t >= 1:
                    pe.wait_ge(s_ra, 4 * t - 2)
                for g in range(2):
                    m = pe.matmul(ps[:, 2, g * S:(g + 1) * S], w_bd[:, g, t, :], xc[:, t, :],
                                  start=True, stop=True)
                m.then_inc(s_gt, 1)

            for c in range(28):
                i, t = c - HEAD0, c - GATE0
                if 0 <= i < HEADS:
                    scores(i)
                if 1 <= i <= HEADS:
                    turn_p(i - 1)
                if 0 <= t < KD:
                    gates(t)
                s, a = c // 2, c % 2
                if c == 0:
                    w = slot(0, 4)
                    pe.wait_ge(s_xlo, 4 * T_IN + 1)
                    for k in range(4):
                        if k < 3:
                            pe.wait_ge(s_lo0, k + 1)
                        else:
                            split(0)
                        m = product(ps[:, 4, :], both(XT, ALL, k, slice(0, P)), both(w, ALL, k, ALL),
                                    k == 0, False)
                    m.then_inc(s_mm, 1)
                    tm_cols_half(0, 0, 4, 1, T_IN)
                    continue
                split(c)
                if s == 0:
                    for h in range(NH):
                        tm_cols_half(c, a, 4, h, T_IN)
                    continue
                if a == 0 and s >= 2:
                    pe.wait_ge(s_slab, 2 * (s - 1))
                if s == 1 and a == 0:
                    pe.wait_ge(s_parc, 1)
                if SLABS[s][0] in FM_SLABS:
                    fm_cols(c, a, slab_banks(s))
                else:
                    tm_cols(c, a, slab_banks(s))
                if 1 <= i <= HEADS:
                    pv(i - 1)

            for n in range(4):
                split(C_AO + n)
                pe.wait_ge(s_olo, 2 * n + 2)
                pe.wait_ge(s_ptc, HEADS)
                tm_rows_half(C_AO + n, OT, 2 * n, 0, n == 0, False, 0)
                pe.wait_ge(s_ra, 4 * KD - 2)
                pe.wait_ge(s_olo, KD)
                tm_rows_half(C_AO + n, OT, 2 * n, 0, n == 0, False, 1)
            for n in range(4):
                split(C_RO + n)
                if n == 0:
                    pe.wait_ge(s_slab, 28)
                pe.wait_ge(s_ylo, 2)
                if n < 3:
                    tm_rows(C_RO + n, XT, 2 * n, 4, n == 0, False)

            def turn_merged(h):
                turn_tile(xn, h, 4, s_xn, 4 + 2 * h)

            last_rows(C_RO + 3, XT, 6, None, 4, turn_merged)
            for n in range(4):
                split(C_WO + n)
                if n < 3:
                    for h in range(NH):
                        if n == 0 and h == 0:
                            pe.wait_ge(s_mrg, 2)
                        pe.wait_ge(s_xlo, 4 * T_MERGE + 2 * h + n // 2 + 1)
                        tm_rows_half(C_WO + n, XT, 2 * n, 0, n == 0, False, h,
                                     (lambda: turn_merged(1)) if n == 0 and h == 0 else None)
            last_rows(C_WO + 3, XT, 6, U_WO)
            feed_forward(0, C_F0, U_WO, T_F0, U_F0)
            feed_forward(1, C_F1, U_F0, T_F1, U_F1)

            def spatial(g):
                pe.wait_ge(s_lv, 6)
                pe.wait_ge(s_ge, 12)
                if g >= 2:
                    pe.wait_ge(s_uv, 2 * (g - 1))
                for h in range(NH):
                    m = pe.matmul(ps[:, 4 + g % 2, h * GW:(h + 1) * GW], ws_t[:, g, :],
                                  g_tm[:, h, g * GW:(g + 1) * GW], start=True, stop=True)
                m.then_inc(s_spa, 1)

            def turn_uv(g):
                pe.wait_ge(s_uv, 2 * g + 2)
                if g >= 2:
                    pe.wait_ge(s_ulo, g - 1)
                for h in range(NH):
                    for t in range(2):
                        m = pe.transpose(ps[:, 6 + g % 2, t * S + h * P:t * S + (h + 1) * P],
                                         uv[:, g % 2, h, t * P:(t + 1) * P], ident[:, :])
                m.then_inc(s_uvT, 1)

            for s in range(8):
                for a in range(2):
                    c = C_AI + 2 * s + a
                    split(c)
                    if a == 0 and s >= 2:
                        pe.wait_ge(s_ge, AI_FREE[s])
                    if s == 0:
                        tm_cols_half(c, a, 4, 0, T_AI, (lambda: turn_x(U_F1, 1)) if a == 0 else None)
                        tm_cols_half(c, a, 4, 1, T_AI)
                    else:
                        tm_cols(c, a, AI_BANKS[s])
                    if (s, a) == (7, 0):
                        turn_uv(0)
                if s == 1:
                    pe.wait_ge(s_wsm, 1)
                    for g in range(NG):
                        m = pe.transpose(ps[:, g // 4, (g % 4) * P:(g % 4 + 1) * P], ws_r[:, g, :],
                                         ident[:, :])
                    m.then_inc(s_wsT, 1)
                if s == 5:
                    pe.wait_ge(s_wsc, 1)
                if s == 6:
                    spatial(0)
                    spatial(1)

            for g in range(NG):
                if g + 2 < NG:
                    spatial(g + 2)
                if g + 1 < NG:
                    turn_uv(g + 1)
                split(C_AW + g)
                pe.wait_ge(s_ulo, g + 1)
                if g == 0:
                    pe.wait_ge(s_ge, 16)
                if g < NG - 1:
                    tm_rows(C_AW + g, OT, 2 * (g % 2), 0, g == 0, False)
                else:
                    last_rows(C_AW + g, OT, 2 * (g % 2), U_AW)
            feed_forward(2, C_F2, U_AW, T_F2, U_F2)

            def keys_and_values():
                for a in range(2):
                    c = C_KV + a
                    split(c)
                    w = slot(c, 4)
                    for t in range(2):
                        for k in range(4):
                            m = product(ps[:, 4, t * S:(t + 1) * S],
                                        both(w, ALL, k, slice(t * P, (t + 1) * P)),
                                        both(XT, ALL, 4 * a + k, ALL),
                                        a == 0 and k == 0 and t == 0, a == 1 and k == 3)
                    m.then_inc(s_mm, 1)
                    if a == 0:
                        token_scale(0)
                    for h in range(NH):
                        for k in range(4):
                            m = product(ps[:, 5, h * 256:(h + 1) * 256],
                                        both(XT, ALL, 4 * a + k, slice(h * P, (h + 1) * P)),
                                        both(w, ALL, k, slice(256, 512)),
                                        a == 0 and k == 0 and h == 0, a == 1 and k == 3)
                    m.then_inc(s_mm, 1)
                pe.wait_ge(s_k, 1)

            def token_scale(n):
                pe.wait_ge(s_diag, 2 * n + 2)
                pe.matmul(ps[:, 0, 0:S], ones[:, :], diag_r[:, :], start=True,
                          stop=True).then_inc(s_R, 1)

            feed_forward(3, C_F3, U_F2, T_F3, U_F3, keys_and_values)

            BLOCKS = ((0, 0), (0, 1), (1, 1))

            def logits(j):
                rows_ = slice(HD * (j % 2), HD * (j % 2) + HD)
                pe.wait_ge(s_q, 2 * (j // 2) + 2)
                if j == 0:
                    pe.wait_ge(s_Rc, 2)
                for b, (sh, th_) in enumerate(BLOCKS):
                    if j >= 1:
                        pe.wait_ge(s_zls, 3 * (j - 1) + b + 1)
                    q = q_b[rows_, 4 * (j // 2):4 * (j // 2) + 4, th_ * P:(th_ + 1) * P]
                    pe.matmul(ps[:, b, :], k_b[rows_, j // 2, sh * P:(sh + 1) * P], q,
                              start=True, stop=True).then_inc(s_z, 1)

            def sums(j):
                pe.wait_ge(s_zm, 2 * j + 2)
                pe.wait_ge(s_zsp, 3 * j + 3)

                def free(b):
                    if j >= 1:
                        pe.wait_ge(s_zd, 3 * (j - 1) + b + 1)

                sp_ = z_sp[:, j % 2, :, :]
                free(0)
                pe.matmul(ps[:, 3, :], later[:, :], sp_[:, 0, :], start=True, stop=True)
                free(1)
                pe.matmul(ps[:, 4, :], later[:, :], sp_[:, 1, :], start=True, stop=False)
                pe.matmul(ps[:, 4, :], ones[:, :], sp_[:, 2, :], start=False, stop=True)
                free(2)
                pe.matmul(ps[:, 5, :], later[:, :], sp_[:, 2, :], start=True,
                          stop=True).then_inc(s_ex, 1)

            def weigh(j):
                pe.wait_ge(s_zam, 2 * j + 2)
                if j == 2:
                    pe.wait_ge(s_zlo, 1)
                rows_ = slice(HD * (j % 2), HD * (j % 2) + HD)
                v = [v_b[:, h, j * HD:(j + 1) * HD] for h in range(NH)]
                a_ = z_a[:, j % 2, :, :]
                pe.matmul(ps[rows_, 6, :], v[0], a_[:, 0, :], start=True, stop=True)
                pe.matmul(ps[rows_, 7, :], v[0], a_[:, 1, :], start=True, stop=False)
                pe.matmul(ps[rows_, 7, :], v[1], a_[:, 2, :], start=False, stop=True).then_inc(s_zo, 1)

            turn_x(U_F3, 1)
            for s in range(2):
                for a in range(2):
                    split(C_Q + 2 * s + a)
                    fm_cols(C_Q + 2 * s + a, a, slab_banks(s), T_Q if s == 0 else None,
                            (lambda: logits(a)) if s == 1 else None)
                    if (s, a) == (0, 0):
                        token_scale(1)
            for j in range(NKV):
                sums(j)
                if j + 2 < NKV:
                    logits(j + 2)
                if j == 1:
                    pe.wait_ge(s_q, 4)
                if j >= 1:
                    weigh(j - 1)

            def b_out(n):
                split(C_BO + n)
                pe.wait_ge(s_zlo, n // 2 + 1)
                if n < 3:
                    tm_rows(C_BO + n, OT, 2 * n, 0, n == 0, False)
                else:
                    last_rows(C_BO + 3, OT, 6, U_BO)

            pe.wait_ge(s_zls, 3 * NKV)
            pe.wait_ge(s_zd, 3 * NKV)
            b_out(0)
            weigh(NKV - 1)
            for n in range(1, 4):
                b_out(n)
            feed_forward(4, C_F4, U_BO, T_F4, U_F4)

        @block.scalar
        def _(act):
            def hi_parts(slot, gains=None):
                if gains is None:
                    act.activation(w_hi[:, slot, :], raw[:, slot, :], ACT.Copy).then_inc(s_hi, 1)
                    return
                for k in range(4):
                    piece = slice(512 * k, 512 * k + 512)
                    m = act.activation(w_hi[:, slot, piece], raw[:, slot, piece], ACT.Copy,
                                       scale=gain(gains[0], gains[1] + k))
                m.then_inc(s_hi, 1)

            def hi(c):
                if c >= N_CHUNKS:
                    return
                act.wait_ge(s_raw[c % RING], 16 * (c // RING + 1))
                if c >= RING:
                    act.wait_ge(s_mm, 2 * (c - RING) + 2)
                hi_parts(c % RING, chunk_gain(c))

            def squares(n, h):
                act.activation(xn[:, h, :], X[:, h, :], ACT.Square,
                               accum_out=ss[:, 2 * n + h:2 * n + h + 1]).then_inc(s_sq, 1)

            def turned(t, h):
                for g in range(2):
                    act.wait_ge(s_turn, 4 * t + 2 * h + g + 1)
                    b = TURN_BASE[t] + 2 * h + g
                    act.activation(xT_hi[:, 4 * g:4 * g + 4, h * P:(h + 1) * P],
                                   ps[:, b, :].rearrange("p (k n) -> p k n", k=4),
                                   ACT.Copy).then_inc(s_xhi, 1)

            def boundary(t, n, u):
                for h in range(NH):
                    turned(t, h)
                    act.wait_ge(s_xup, 4 * u + 2 * h + 2)
                    act.wait_ge(s_sq, 2 * n)
                    squares(n, h)

            def feed_forward(f, c0, n, after_first=None):
                j0 = f * NJ

                def h_hi(j, t0=0):
                    act.wait_ge(s_hT, j + 1)
                    act.activation(oT_hi[:, t0:t0 + 2, :],
                                   ps[:, 6, :].rearrange("p (t s) -> p t s", t=2), ACT.Copy).then_inc(s_hhi, 1)

                def gate(c, j, banks=4):
                    for h in range(NH):
                        act.wait_ge(s_mm, c * 2 + (h + 1))
                        i = 2 * n + h
                        act.activation(silu[:, h, :], ps[:, banks + h, 0:GW], ACT.Silu,
                                       scale=rstd[:, i:i + 1]).then_inc(s_silu, 1)

                def next_hi(m, i, gains=None):
                    slot = (c0 + m) % RING
                    act.wait_ge(s_raw[slot], i * 16 + 16 * ((c0 + m + RING) // RING + 1))
                    act.wait_ge(s_mm, i * 6 + (2 * (c0 + m) + 2))
                    hi_parts(slot, gains)

                hi(c0 + 3)
                act.wait_ge(s_rstd, 2 * n + 2)
                gate(c0 + 1, j0, 6)
                hi(c0 + 4)
                if after_first is not None:
                    after_first()
                    c0 += 2
                h_hi(j0)
                hi(c0 + 5)
                gate(c0 + 3, j0 + 1)
                hi(c0 + 6)
                hi(c0 + 7)
                g = chunk_gain(c0 + 5)[0]
                with act.Fori(0, NJ - 3) as i:
                    h_hi(i + (j0 + 1))
                    next_hi(5, i, (g, 0))
                    gate(i * 3 + (c0 + 6), i + (j0 + 2))
                    next_hi(6, i, (g, 4))
                    next_hi(7, i)
                e = c0 + 3 * NJ - 1
                j = j0 + NJ - 1
                h_hi(j - 1)
                hi(e)
                gate(e - 2, j)
                hi(e + 1)
                h_hi(j, 2)
                hi(e + 2)

            act.preload_act_table_set("exp_and_others")
            for h in range(NH):
                act.wait_ge(s_x[h], 16)
                squares(N_IN, h)
            turned(T_IN, 0)
            act.wait_ge(s_parc, 1)
            act.wait_ge(s_raw[0], 16)
            for k in range(4):
                piece = slice(512 * k, 512 * k + 512)
                act.activation(w_hi[:, 0, piece], raw[:, 0, piece], ACT.Copy,
                               scale=gain(G_IN, k)).then_inc(s_hi0 if k < 3 else s_hi, 1)
            turned(T_IN, 1)
            hi(1)
            act.wait_ge(s_sp, 1)
            act.activation(spt[:, 1, :], spt[:, 0, :], ACT.Exp, scale=-1.0).then_inc(s_spe, 1)

            def band_exp(i):
                act.wait_ge(s_max, 2 * i + 2)
                for h, (c0, n) in enumerate(((0, P), (P, S))):
                    act.activation(sbuf_s[:, i % 2, c0:c0 + n], sbuf_s[:, i % 2, c0:c0 + n], ACT.Exp,
                                   bias=stat[:, i % 2, h:h + 1],
                                   accum_out=stat[:, i % 2, 2 + h:3 + h]).then_inc(s_exp, 1)

            def copy_p(i):
                act.wait_ge(s_pt, i + 1)
                act.activation(pT[:, i % 2, :], ps[:, i % 2, 0:384], ACT.Copy).then_inc(s_ptc, 1)

            def o_hi(t):
                act.wait_ge(s_pv, 2 * t + 2)
                act.activation(oT_hi[:, t, :], ps[:, 3, 0:S],
                               ACT.Copy).then_inc(s_ohi, 1)

            def gate_functions(t):
                act.wait_ge(s_gt, t + 1)
                if t == 0:
                    act.wait_ge(s_sp, SP_DONE)
                if t >= 1:
                    act.wait_ge(s_rd, 3 * t)
                for g in range(2):
                    act.activation(rg_t[:, g, :], ps[:, 2, g * S:(g + 1) * S], ACT.Tanh, scale=0.5,
                                   bias=half_b[:, 8 * g + t:8 * g + t + 1]).then_inc(s_ra, 1)
                act.wait_ge(s_ra, 4 * t + 2)
                act.activation(xrp[:, t, 3:3 + S], rg_t[:, 0, :], ACT.Exp, scale=sp4[:, 8 + t:9 + t],
                               bias=sp4[:, 8 + t:9 + t]).then_inc(s_ra, 1)
                act.activation(th[:, t, :], rg_t[:, 0, :], ACT.Tanh, scale=sp4[:, t:t + 1],
                               bias=sp4[:, t:t + 1]).then_inc(s_ra, 1)

            for c in range(28):
                i, t = c - HEAD0, c - GATE0
                if 2 <= i <= HEADS + 1 and i % 2:
                    o_hi((i - 2) // 2)
                hi(c + 2)
                if 1 <= i <= HEADS:
                    copy_p(i - 1)
                if 0 <= i < HEADS:
                    band_exp(i)
                if 0 <= t < KD:
                    gate_functions(t)
                if c % 2:
                    s = c // 2
                    kind, n = SLABS[s]
                    banks = slab_banks(s)
                    for h in range(NH):
                        src = ps[:, banks + h, :]
                        if kind in ("ga", "gb"):
                            act.wait_ge(s_bsum, 2 * (s - 10) + h + 1)
                            dst = qk[:, s - 10, h * 512:(h + 1) * 512]
                            act.activation(dst, dst, ACT.Tanh, scale=0.5).then_inc(s_slab, 1)
                            continue
                        act.wait_ge(s_mm, 2 * c + h + 1)
                        if kind == "xr":
                            act.wait_ge(s_z0, 2)
                            act.activation(xrp[:, 4 * n + 2 * h:4 * n + 2 * h + 2, 3:3 + S],
                                           src.rearrange("p (t s) -> p t s", t=2),
                                           ACT.Copy).then_inc(s_slab, 1)
                            continue
                        if kind == "gr":
                            dst = gr[:, 4 * n + 2 * h:4 * n + 2 * h + 2, :].rearrange("p t s -> p (t s)")
                        elif kind == "v":
                            dst = v_tm[:, h, n * 512:(n + 1) * 512]
                        else:
                            dst = qk[:, 2 * n + (kind == "k"), h * 512:(h + 1) * 512]
                        fn = ACT.Gelu_apprx_tanh if kind == "gr" else ACT.Copy
                        act.activation(dst, src, fn).then_inc(s_slab, 1)
            o_hi(KD - 1)
            hi(C_AO + 2)

            act.wait_ge(s_rd, 3 * KD)
            act.activation(th[:, :, :], th[:, :, :], ACT.Sqrt, scale=0.25).then_inc(s_sqrt, 1)
            for n in range(4):
                if n == 0:
                    hi(C_AO + n + RING)
                    act.wait_ge(s_mm, 2 * C_AO)
                    for h in range(2):
                        act.wait_ge(s_y, h + 1)
                        act.activation(xT_hi[:, 4 * h:4 * h + 4, :], xc[:, 4 * h:4 * h + 4, :],
                                       ACT.Copy).then_inc(s_yhi, 1)
                else:
                    hi(C_AO + n + RING)
            for n in range(3):
                hi(C_RO + n + RING)
            for h in range(NH):
                turned(T_MERGE, h)
            hi(C_WO + 2)
            for n in range(3):
                hi(C_WO + n + RING)
            boundary(T_F0, N_F0, U_WO)
            hi(C_F0 + 2)
            act.wait_ge(s_gf, 1)
            feed_forward(0, C_F0, N_F0)
            boundary(T_F1, N_END1, U_F0)
            hi(C_F1 + 2)
            for h in range(NH):
                act.wait_ge(s_xg, h + 1)
                act.wait_ge(s_sq, 2 * N_F1)
                squares(N_F1, h)
            feed_forward(1, C_F1, N_F1)

            boundary(T_AI, N_AI, U_F1)
            hi(C_AI + 2)

            def uv_hi(g):
                act.wait_ge(s_uvT, g + 1)
                if g >= 2:
                    act.wait_ge(s_mm, 2 * (C_AW + g - 2) + 2)
                act.activation(oT_hi[:, 2 * (g % 2):2 * (g % 2) + 2, :],
                               ps[:, 6 + g % 2, :].rearrange("p (t s) -> p t s", t=2),
                               ACT.Copy).then_inc(s_uhi, 1)

            for s in range(8):
                for a in range(2):
                    c = C_AI + 2 * s + a
                    if a:
                        if s == 0:
                            act.wait_ge(s_rstd, 2 * N_AI + 2)
                        for h in range(NH):
                            act.wait_ge(s_mm, 2 * c + h + 1)
                            dst = g_tm if s < 4 else u_tm
                            i = 2 * N_AI + h
                            act.activation(dst[:, h, 512 * (s % 4):512 * (s % 4 + 1)],
                                           ps[:, AI_BANKS[s] + h, :], ACT.Gelu_apprx_tanh,
                                           scale=rstd[:, i:i + 1]).then_inc(s_ge, 1)
                    if (s, a) == (2, 0):
                        act.wait_ge(s_wsT, 1)
                        act.activation(ws_t, ps[:, 0:2, :].rearrange("p b (g s) -> p (b g) s", s=P),
                                       ACT.Copy).then_inc(s_wsc, 1)
                    hi(c + RING)
                    if (s, a) == (7, 0):
                        uv_hi(0)

            for g in range(NG - 1):
                uv_hi(g + 1)
                hi(C_AW + g + RING)
            boundary(T_F2, N_F2, U_AW)
            hi(C_F2 + 2)
            feed_forward(2, C_F2, N_F2)

            def copy_R(n):
                act.wait_ge(s_R, n + 1)
                act.activation(R[:, :], ps[:, 0, 0:S], ACT.Copy).then_inc(s_Rc, 1)

            def values():
                copy_R(0)
                hi(C_KV + RING)
                act.wait_ge(s_mm, 2 * (C_KV + 1) + 2)
                for h in range(NH):
                    i = 2 * N_F3 + h
                    act.activation(v_b[:, h, :], ps[:, 5, h * 256:(h + 1) * 256], ACT.Copy,
                                   scale=rstd[:, i:i + 1]).then_inc(s_v, 1)
                hi(C_KV + 1 + RING)

            boundary(T_F3, N_F3, U_F2)
            hi(C_F3 + 2)
            feed_forward(3, C_F3, N_F3, values)
            boundary(T_Q, N_Q, U_F3)
            hi(C_Q + 2)
            copy_R(1)
            hi(C_Q + 3)
            act.preload_act_table_set("natural_log_exp_and_others")

            def z_magnitude(j):
                for b in range(3):
                    act.wait_ge(s_z, 3 * j + b + 1)
                    if j >= 2:
                        act.wait_ge(s_zls, 3 * (j - 2) + b + 1)
                    act.activation(z_abs[:, j % 2, b, :], ps[:, b, :], ACT.Abs).then_inc(s_ab, 1)

            def log_part(j):
                for b in range(3):
                    t = z_abs[:, j % 2, b, :]
                    act.wait_ge(s_ab, 3 * j + b + 1)
                    act.activation(t, t, ACT.Exp, scale=-1.0).then_inc(s_ze, 1)
                for b in range(3):
                    t = z_abs[:, j % 2, b, :]
                    act.wait_ge(s_ze, 3 * j + b + 1)
                    act.activation(t, t, ACT.Ln, bias=1.0).then_inc(s_zl, 1)

            def weights(j):
                act.wait_ge(s_zd, 3 * j + 3)
                if j >= 2:
                    act.wait_ge(s_zo, j - 1)
                act.activation(z_a[:, j % 2, :, :], z_ls[:, j % 2, :, :], ACT.Exp).then_inc(s_za, 1)

            def z_hi(m):
                act.wait_ge(s_zo, 2 * m + 2)
                act.activation(oT_hi[:, 4 * m:4 * m + 4, :].rearrange("p g (h t) -> p h g t", h=NH),
                               ps[:, 6:8, :].rearrange("p h (g t) -> p h g t", g=GRP),
                               ACT.Copy).then_inc(s_zhi, 1)

            hi(C_Q + 4)
            z_magnitude(0)
            log_part(0)
            hi(C_Q + 5)
            z_magnitude(1)
            log_part(1)
            z_magnitude(2)
            weights(0)
            log_part(2)
            z_magnitude(3)
            weights(1)
            log_part(3)
            weights(2)
            z_hi(0)
            hi(C_Q + 6)
            weights(3)
            hi(C_BO + RING)
            z_hi(1)
            for n in range(1, 3):
                hi(C_BO + n + RING)
            boundary(T_F4, N_F4, U_BO)
            hi(C_F4 + 2)
            feed_forward(4, C_F4, N_F4)
            for h in range(NH):
                act.wait_ge(s_xup, 4 * U_F4 + 2 * h + 2)
                act.wait_ge(s_sq, 2 * N_END2)
                squares(N_END2, h)

        @block.vector
        def _(dve):
            def lo_parts(slot, gains=None, k0=0, k1=4):
                if gains is None:
                    piece = slice(512 * k0, 512 * k1)
                    m = dve.tensor_tensor(w_lo[:, slot, piece], raw[:, slot, piece],
                                          f32(w_hi[:, slot, piece]), ALU.subtract)
                else:
                    for k in range(k0, k1):
                        piece = slice(512 * k, 512 * k + 512)
                        m = dve.scalar_tensor_tensor(out=w_lo[:, slot, piece], in0=raw[:, slot, piece],
                                                     scalar=gain(gains[0], gains[1] + k),
                                                     in1=f32(w_hi[:, slot, piece]),
                                                     op0=ALU.mult, op1=ALU.subtract)
                if k1 == 4:
                    m.then_inc(s_lo, 1)

            def lo(c, k0=0, k1=4):
                if c >= N_CHUNKS:
                    return
                dve.wait_ge(s_hi, c + 1)
                lo_parts(c % RING, chunk_gain(c), k0, k1)

            def turned(t, h):
                for g in range(2):
                    dve.wait_ge(s_xhi, 4 * t + 2 * h + g + 1)
                    x = (slice(None), slice(4 * g, 4 * g + 4), slice(h * P, (h + 1) * P))
                    b = TURN_BASE[t] + 2 * h + g
                    dve.tensor_tensor(xT_lo[x], ps[:, b, :].rearrange("p (k n) -> p k n", k=4),
                                      f32(xT_hi[x]), ALU.subtract).then_inc(s_xlo, 1)

            def computed(c, u, h, n):
                if n == 0:
                    dve.wait_ge(s_half, 2 * (u - U_MERGE) + h + 1)
                else:
                    dve.wait_ge(s_mm, 2 * c + h + 1)

            def update(c, u, scale, h):
                for n in range(2):
                    computed(c, u, h, n)
                    x = X[:, h, n * 512:(n + 1) * 512]
                    dve.scalar_tensor_tensor(out=x, in0=ps[:, 2 * h + n, :], scalar=scale, in1=x,
                                             op0=ALU.mult, op1=ALU.add).then_inc(s_xup, 1)

            def boundary(e, u, scale, t, change=None):
                for h in range(NH):
                    if change is None:
                        update(e, u, scale, h)
                    else:
                        change(h)
                    if t != T_Q:
                        lo(e + 2, 2 * h, 2 * h + 2)
                    turned(t, h)
                if t == T_Q:
                    lo(e + 2)

            def feed_forward(f, c0, n, after_first=None, extra=None):
                j0 = f * NJ

                def h_lo(j, t0=0):
                    dve.wait_ge(s_hhi, j + 1)
                    dve.tensor_tensor(oT_lo[:, t0:t0 + 2, :],
                                      ps[:, 6, :].rearrange("p (t s) -> p t s", t=2),
                                      f32(oT_hi[:, t0:t0 + 2, :]), ALU.subtract).then_inc(s_hlo, 1)

                def gated(j, banks=4):
                    for h in range(NH):
                        dve.wait_ge(s_silu, j * 2 + (h + 1))
                        i = 2 * n + h
                        dve.scalar_tensor_tensor(out=h_tm[:, h, :], in0=ps[:, banks + h, GW:2 * GW],
                                                 scalar=rstd[:, i:i + 1], in1=silu[:, h, :],
                                                 op0=ALU.mult, op1=ALU.mult).then_inc(s_h, 1)

                def next_lo(m, i, gains=None):
                    slot = (c0 + m) % RING
                    dve.wait_ge(s_hi, i * 3 + (c0 + m + RING + 1))
                    lo_parts(slot, gains)

                lo(c0 + 3)
                if extra is not None:
                    extra()
                gated(j0, 6)
                lo(c0 + 4)
                if after_first is not None:
                    after_first()
                    c0 += 2
                h_lo(j0)
                lo(c0 + 5)
                gated(j0 + 1)
                lo(c0 + 6)
                lo(c0 + 7)
                g = chunk_gain(c0 + 5)[0]
                with dve.Fori(0, NJ - 3) as i:
                    h_lo(i + (j0 + 1))
                    next_lo(5, i, (g, 0))
                    gated(i + (j0 + 2))
                    next_lo(6, i, (g, 4))
                    next_lo(7, i)
                e = c0 + 3 * NJ - 1
                j = j0 + NJ - 1
                h_lo(j - 1)
                lo(e)
                gated(j)
                lo(e + 1, 0, 1)
                h_lo(j, 2)
                lo(e + 1, 1, 4)

            def diag_rstd(n, m):
                if m:
                    dve.wait_ge(s_R, m)
                dve.wait_ge(s_rstd, 2 * n + 2)
                for h in range(NH):
                    i = 2 * n + h
                    dve.tensor_scalar(diag_r[:, h * P:(h + 1) * P], ident[:, :], rstd[:, i:i + 1],
                                      None, ALU.mult).then_inc(s_diag, 1)

            dve.wait_ge(s_parT, 1)
            dve.tensor_copy(cols[:, :], ps[:, 7, 0:2 * P]).then_inc(s_parc, 1)
            for h in range(NH):
                i = 2 * N_IN + h
                dve.wait_ge(s_rstd, i + 1)
                for n in range(2):
                    cols_ = slice(n * 512, (n + 1) * 512)
                    dve.tensor_scalar(xn[:, h, cols_], X[:, h, cols_], rstd[:, i:i + 1], None,
                                      ALU.mult).then_inc(s_xn, 1)
            turned(T_IN, 0)
            for k in range(4):
                piece = slice(512 * k, 512 * k + 512)
                dve.wait_ge(*((s_hi0, k + 1) if k < 3 else (s_hi, 1)))
                dve.scalar_tensor_tensor(out=w_lo[:, 0, piece], in0=raw[:, 0, piece],
                                         scalar=gain(G_IN, k), in1=f32(w_hi[:, 0, piece]),
                                         op0=ALU.mult, op1=ALU.subtract
                                         ).then_inc(s_lo0 if k < 3 else s_lo, 1)
            turned(T_IN, 1)
            lo(1)
            dve.tensor_tensor(g_f1[:, :], cols[:, G_F1:G_F1 + KD], cols[:, G_END1:G_END1 + KD],
                              ALU.mult).then_inc(s_gf, 1)
            dve.wait_ge(s_parc, 1)
            lam = par[:, 56:64]
            neg, e, den, r, r2, t_ = (spt[:, i, :] for i in range(6))
            dve.scalar_tensor_tensor(out=neg, in0=lam, scalar=-1.0, in1=lam, op0=ALU.mult,
                                     op1=ALU.max).then_inc(s_sp, 1)
            steps = [1]

            def step(ins):
                steps[0] += 1
                ins.then_inc(s_sp, 1)
                dve.wait_ge(s_sp, steps[0])

            def softplus_lambda():
                dve.wait_ge(s_spe, 1)
                step(dve.tensor_scalar(den, e, 2.0, None, ALU.add))
                step(dve.reciprocal(den, den))
                step(dve.tensor_tensor(r, e, den, ALU.mult))
                step(dve.tensor_tensor(r2, r, r, ALU.mult))
                step(dve.tensor_scalar(t_, r2, 1.0 / 17, None, ALU.mult))
                for k in (15, 13, 11, 9, 7, 5, 3):
                    step(dve.scalar_tensor_tensor(out=t_, in0=t_, scalar=1.0 / k, in1=r2,
                                                  op0=ALU.add, op1=ALU.mult))
                step(dve.scalar_tensor_tensor(out=t_, in0=t_, scalar=1.0, in1=r, op0=ALU.add,
                                              op1=ALU.mult))
                step(dve.tensor_scalar(neg, lam, -1.0, 0.0, ALU.mult, ALU.max))
                step(dve.scalar_tensor_tensor(out=t_, in0=t_, scalar=2.0, in1=neg, op0=ALU.mult,
                                              op1=ALU.add))
                step(dve.tensor_scalar(sp4[:, 0:8], t_, 4.0, None, ALU.mult))
                step(dve.tensor_scalar(sp4[:, 8:16], t_, -4.0, None, ALU.mult))
                step(dve.tensor_scalar(half_b[:, :], par[:, 40:56], 0.5, None, ALU.mult))
                assert steps[0] == SP_DONE


            def band_scores(i):
                dve.wait_ge(s_sc, i + 1)
                dve.wait_ge(s_mask, i + 1)
                dve.scalar_tensor_tensor(out=sbuf_s[:, i % 2, :], in0=ps[:, i % 2, 0:384],
                                         scalar=HD ** -0.5, in1=bias_t[:, i % 3, :],
                                         op0=ALU.mult, op1=ALU.add).then_inc(s_sb, 1)
                dve.wait_ge(s_sb, i + 1)
                for h, (c0, n) in enumerate(((0, P), (P, S))):
                    dve.tensor_reduce(stat[:, i % 2, h:h + 1], sbuf_s[:, i % 2, c0:c0 + n], AX, ALU.max,
                                      negate=True).then_inc(s_max, 1)

            def band_norm(i):
                dve.wait_ge(s_exp, 2 * i + 2)
                dve.reciprocal(stat[:, i % 2, 2:4], stat[:, i % 2, 2:4]).then_inc(s_rec, 1)
                dve.wait_ge(s_rec, i + 1)
                for h, (c0, n) in enumerate(((0, P), (P, S))):
                    dve.tensor_scalar(sbuf_s[:, i % 2, c0:c0 + n], sbuf_s[:, i % 2, c0:c0 + n],
                                      stat[:, i % 2, 2 + h:3 + h], None, ALU.mult).then_inc(s_pn, 1)

            def o_lo(t):
                dve.wait_ge(s_ohi, t + 1)
                dve.tensor_tensor(oT_lo[:, t, :], ps[:, 3, 0:S],
                                  f32(oT_hi[:, t, :]), ALU.subtract).then_inc(s_olo, 1)

            def convolve(t):
                dve.wait_ge(s_slab, SLAB_AT["xr", t // 4])
                dve.tensor_scalar(xc[:, t, :], xrp[:, t, 3:3 + S], par[:, 24 + t:25 + t],
                                  par[:, 32 + t:33 + t], ALU.mult, ALU.add).then_inc(s_cv, 1)
                for n in range(1, 4):
                    dve.wait_ge(s_cv, 4 * t + n)
                    w = 8 * (3 - n) + t
                    dve.scalar_tensor_tensor(out=xc[:, t, :], in0=xrp[:, t, 3 - n:3 - n + S],
                                             scalar=par[:, w:w + 1], in1=xc[:, t, :],
                                             op0=ALU.mult, op1=ALU.add).then_inc(s_cv, 1)

            def gate_products(t):
                dve.wait_ge(s_ra, 4 * t + 4)
                dve.scalar_tensor_tensor(out=xc[:, t, :], in0=rg_t[:, 1, :], scalar=1.0,
                                         in1=xc[:, t, :], op0=ALU.add, op1=ALU.mult).then_inc(s_rd, 1)
                dve.tensor_tensor(rg_t[:, 2, :], xrp[:, t, 3:3 + S], xrp[:, t, 3:3 + S],
                                  ALU.mult).then_inc(s_rd, 1)
                dve.wait_ge(s_rd, 3 * t + 2)
                dve.scalar_tensor_tensor(out=th[:, t, :], in0=rg_t[:, 2, :], scalar=1.0,
                                         in1=th[:, t, :], op0=ALU.add, op1=ALU.mult).then_inc(s_rd, 1)

            for c in range(28):
                i, t = c - HEAD0, c - GATE0
                if 0 <= i < HEADS:
                    band_scores(i)
                if 2 <= i <= HEADS + 1 and i % 2:
                    o_lo((i - 2) // 2)
                if 0 <= t + 1 < KD:
                    convolve(t + 1)
                lo(c + 2)
                if c == 1:
                    softplus_lambda()
                if 0 <= i < HEADS:
                    band_norm(i)
                if 0 <= t < KD:
                    gate_products(t)
                s, a = c // 2, c % 2
                if a and s >= 10:
                    dve.wait_ge(s_sc, (8, 8, 16, 16)[s - 10])
                    dve.wait_ge(s_bm[s % 2], 16 * ((s - 10) // 2 + 1))
                    for h in range(NH):
                        dve.wait_ge(s_mm, 2 * c + h + 1)
                        dve.tensor_tensor(qk[:, s - 10, h * 512:(h + 1) * 512],
                                          ps[:, slab_banks(s) + h, :],
                                          row_b[:, (s % 2) * 512:(s % 2 + 1) * 512],
                                          ALU.add).then_inc(s_bsum, 1)
            o_lo(KD - 1)
            lo(C_AO + 2)

            dve.wait_ge(s_sqrt, 1)
            dve.tensor_tensor(xc[:, :, :], th[:, :, :], xc[:, :, :], ALU.mult).then_inc(s_bx, 1)
            dve.wait_ge(s_bx, 1)
            for t in range(KD):
                dve.tensor_tensor_scan(th[:, t, :], xrp[:, t, 3:3 + S], xc[:, t, :], 0.0,
                                       ALU.mult, ALU.add).then_inc(s_scan, 1)
            lo(C_AO + RING)
            for h in range(2):
                dve.wait_ge(s_scan, 4 * h + 4)
                tiles = slice(4 * h, 4 * h + 4)
                dve.tensor_tensor(xc[:, tiles, :], th[:, tiles, :], gr[:, tiles, :],
                                  ALU.mult).then_inc(s_y, 1)
            for h in range(2):
                tiles = slice(4 * h, 4 * h + 4)
                dve.wait_ge(s_yhi, h + 1)
                dve.tensor_tensor(xT_lo[:, tiles, :], xc[:, tiles, :], f32(xT_hi[:, tiles, :]),
                                  ALU.subtract).then_inc(s_ylo, 1)
            for n in range(1, 4):
                lo(C_AO + n + RING)

            ya = v_tm
            dve.wait_ge(s_slab, 28)
            for h in range(NH):
                dve.wait_ge(s_mm, 2 * (C_AO + 3) + h + 1)
                dve.scalar_tensor_tensor(out=ya[:, h, :].rearrange("p (a n) -> p a n", a=2),
                                         in0=qk[:, 0:2, h * 512:(h + 1) * 512], scalar=1.0,
                                         in1=ps[:, 2 * h:2 * h + 2, :], op0=ALU.add,
                                         op1=ALU.mult).then_inc(s_mrg, 1)
            for n in range(2):
                lo(C_RO + n + RING)

            def merged(h):
                for n in range(2):
                    computed(C_RO + 3, U_MERGE, h, n)
                    cols_ = slice(n * 512, (n + 1) * 512)
                    t = xn[:, h, cols_]
                    dve.scalar_tensor_tensor(out=t, in0=qk[:, 2 + n, h * 512:(h + 1) * 512],
                                             scalar=1.0, in1=ps[:, 4 + 2 * h + n, :],
                                             op0=ALU.add, op1=ALU.mult).then_inc(s_mrg, 1)
                    dve.wait_ge(s_mrg, 3 + 2 * h + n)
                    dve.tensor_tensor(t, t, ya[:, h, cols_], ALU.add).then_inc(s_xn, 1)

            boundary(C_RO + 3, U_MERGE, None, T_MERGE, merged)
            lo(C_WO + 2)
            for n in range(2):
                lo(C_WO + n + RING)
            boundary(C_WO + 3, U_WO, 0.5, T_F0)
            lo(C_F0 + 2)
            dve.wait_ge(s_gf, 1)
            feed_forward(0, C_F0, N_F0)
            boundary(C_F1 - 1, U_F0, 1.0, T_F1)
            dve.wait_ge(s_g1, 16)
            for h in range(NH):
                dve.wait_ge(s_sq, 2 * N_END1 + h + 1)
                dve.tensor_tensor(X[:, h, :], X[:, h, :], row_b[:, :], ALU.mult).then_inc(s_xg, 1)
            lo(C_F1 + 2)

            def finish_end1():
                for h in range(NH):
                    dve.wait_ge(s_sq, 2 * N_F1 + h + 1)
                    i = 2 * N_END1 + h
                    dve.wait_ge(s_rstd, i + 1)
                    dve.tensor_scalar(X[:, h, :], X[:, h, :], rstd[:, i:i + 1], None,
                                      ALU.mult).then_inc(s_xg, 1)

            feed_forward(1, C_F1, N_F1, None, finish_end1)
            dve.wait_ge(s_xg, 4)
            boundary(C_AI - 1, U_F1, 0.5, T_AI)
            lo(C_AI + 2)

            def gated(g):
                dve.wait_ge(s_ge, 2 * (4 + g // 2) + 2)
                dve.wait_ge(s_spa, g + 1)
                if g >= 2:
                    dve.wait_ge(s_uvT, g - 1)
                for h in range(NH):
                    dve.scalar_tensor_tensor(out=uv[:, g % 2, h, :],
                                             in0=ps[:, 4 + g % 2, h * GW:(h + 1) * GW],
                                             scalar=par[:, 64 + g:65 + g],
                                             in1=u_tm[:, h, g * GW:(g + 1) * GW],
                                             op0=ALU.add, op1=ALU.mult).then_inc(s_uv, 1)

            def uv_lo(g):
                dve.wait_ge(s_uhi, g + 1)
                t = (slice(None), slice(2 * (g % 2), 2 * (g % 2) + 2), slice(None))
                dve.tensor_tensor(oT_lo[t], ps[:, 6 + g % 2, :].rearrange("p (t s) -> p t s", t=2),
                                  f32(oT_hi[t]), ALU.subtract).then_inc(s_ulo, 1)

            for s in range(8):
                if s == 7:
                    gated(0)
                    gated(1)
                if s in (4, 5):
                    h = s - 4
                    dve.wait_ge(s_ln, 32)
                    dve.wait_ge(s_lrs, h + 1)
                    dve.tensor_scalar(g_tm[:, h, :], g_tm[:, h, :], mv[:, h, 0:1], ln_rs[:, h, 1:2],
                                      ALU.subtract, ALU.mult).then_inc(s_lv, 1)
                    dve.wait_ge(s_lv, 3 * h + 1)
                    dve.tensor_tensor(g_tm[:, h, :], g_tm[:, h, :], ln_g, ALU.mult).then_inc(s_lv, 1)
                lo(C_AI + 2 * s + RING)
                if s in (4, 5):
                    dve.wait_ge(s_lv, 3 * h + 2)
                    dve.tensor_tensor(g_tm[:, h, :], g_tm[:, h, :], ln_b, ALU.add).then_inc(s_lv, 1)
                if s == 7:
                    uv_lo(0)
                lo(C_AI + 2 * s + 1 + RING)
                if s < 4:
                    for h in range(NH):
                        dve.wait_ge(s_ge, 2 * s + h + 1)
                        dve.bn_stats(bn[:, h, s, :], g_tm[:, h, 512 * s:512 * (s + 1)]).then_inc(s_bn, 1)
                if s == 3:
                    dve.wait_ge(s_bn, 8)
                    for h in range(NH):
                        dve.bn_aggr(mv[:, h, :], bn[:, h, :, :]).then_inc(s_mv, 1)

            for g in range(NG):
                if g + 2 < NG:
                    gated(g + 2)
                if g + 1 < NG:
                    uv_lo(g + 1)
                if g < NG - 2:
                    lo(C_AW + g + RING)
            boundary(C_F2 - 1, U_AW, 1.0, T_F2)
            lo(C_F2 + 2)
            feed_forward(2, C_F2, N_F2)

            def keys():
                dve.wait_ge(s_Rc, 1)
                dve.wait_ge(s_mm, 2 * (C_KV + 1) + 1)
                dve.tensor_tensor(k_b, ps[:, 4, :].rearrange("p (t s) -> p t s", t=2), R_of(2),
                                  ALU.mult).then_inc(s_k, 1)
                lo(C_KV + RING)
                lo(C_KV + 1 + RING)

            def R_of(n):
                return R[:, :].rearrange("p (o s) -> p o s", o=1).broadcast_to([P, n, S])

            boundary(C_F3 - 1, U_F2, 0.5, T_F3)
            lo(C_F3 + 2)
            feed_forward(3, C_F3, N_F3, keys, lambda: diag_rstd(N_F3, 0))
            boundary(C_Q - 1, U_F3, 0.5, T_Q)
            diag_rstd(N_Q, 1)
            lo(C_Q + 2)
            lo(C_Q + 3)

            def queries(s):
                for h in range(2):
                    dve.wait_ge(s_mm, 2 * (C_Q + 2 * s + 1) + h + 1)
                    dve.wait_ge(s_Rc, 2)
                    dve.scalar_tensor_tensor(out=q_b[:, 4 * s + 2 * h:4 * s + 2 * h + 2, :],
                                             in0=ps[:, slab_banks(s) + h, :]
                                             .rearrange("p (t s) -> p t s", t=2),
                                             scalar=HD ** -0.5, in1=R_of(2), op0=ALU.mult,
                                             op1=ALU.mult).then_inc(s_q, 1)

            def softplus(j):
                if j >= 2:
                    dve.wait_ge(s_ex, j - 1)
                    dve.wait_ge(s_za, j - 1)
                for b in range(3):
                    z, L = ps[:, b, :], z_abs[:, j % 2, b, :]
                    dve.wait_ge(s_zl, 3 * j + b + 1)
                    dve.scalar_tensor_tensor(out=z_sp[:, j % 2, b, :], in0=z, scalar=0.0, in1=L,
                                             op0=ALU.max, op1=ALU.add).then_inc(s_zsp, 1)
                    dve.scalar_tensor_tensor(out=z_ls[:, j % 2, b, :], in0=z, scalar=0.0, in1=L,
                                             op0=ALU.min, op1=ALU.subtract).then_inc(s_zls, 1)

            def exponent(j):
                dve.wait_ge(s_ex, j + 1)
                dve.wait_ge(s_zls, 3 * j + 3)
                for b in range(3):
                    t = z_ls[:, j % 2, b, :]
                    dve.tensor_tensor(t, t, ps[:, 3 + b, :], ALU.subtract).then_inc(s_zd, 1)

            def z_lo(m):
                dve.wait_ge(s_zhi, m + 1)
                for h in range(NH):
                    t = (slice(None), slice(4 * m, 4 * m + 4), slice(h * P, (h + 1) * P))
                    ins = dve.tensor_tensor(oT_lo[t], ps[:, 6 + h, :].rearrange("p (g t) -> p g t", g=GRP),
                                            f32(oT_hi[t]), ALU.subtract)
                ins.then_inc(s_zlo, 1)

            queries(0)
            lo(C_Q + 4)
            softplus(0)
            lo(C_Q + 5)
            queries(1)
            softplus(1)
            exponent(0)
            softplus(2)
            exponent(1)
            softplus(3)
            exponent(2)
            z_lo(0)
            exponent(3)
            lo(C_Q + 6)
            lo(C_BO + RING)
            z_lo(1)
            lo(C_BO + 1 + RING)
            boundary(C_F4 - 1, U_BO, 1.0, T_F4)
            lo(C_F4 + 2)
            feed_forward(4, C_F4, N_F4)
            dve.wait_ge(s_g2, 16)
            for h in range(NH):
                update(N_CHUNKS - 1, U_F4, 0.5, h)
            for h in range(NH):
                i = 2 * N_END2 + h
                dve.wait_ge(s_rstd, i + 1)
                dve.scalar_tensor_tensor(out=xn[:, h, :], in0=X[:, h, :], scalar=rstd[:, i:i + 1],
                                         in1=row_b[:, :], op0=ALU.mult,
                                         op1=ALU.mult).then_inc(s_xn, 1)
    return nc


SP_DONE = 19
XN_END = 8
AI_BANKS = (4, 6, 4, 6, 4, 6, 0, 2)
AI_FREE = (0, 0, 2, 4, 6, 8, 4, 4)
SLAB_AT = {s: 2 * (n + 1) for n, s in enumerate(SLABS)}
TURN_BASE = (0, 4, 0, 0, 0, 0, 0, 0, 0)

_INS = ["x", "stream", "params", "b_merge", "rel_rev", "w_rg_r", "w_rg_i", "final_norm_g",
        "a_ln_g_2", "a_ln_b_2", "a_w_s_2", "final_norm_2"]
_ONE_LAYER = ("norm_mix_g", "w_in", "b_merge", "rel_table", "w_attn_out", "conv_w", "conv_b",
              "w_rg_r", "b_rg_r", "w_rg_i", "b_rg_i", "rg_lambda", "w_rnn_out", "w_o", "norm_ffn_g",
              "w_ffn_in", "w_ffn_out", "a_w_in_2", "a_ln_g_2", "a_ln_b_2", "a_w_s_2",
              "a_b_s_2", "a_w_out_2", "b_w_q_2", "b_w_o_2", "x")


def _stream(w):
    import numpy as _np

    chunks = []

    def columns(m, col, width=512):
        t = m.reshape(2, 4, P, m.shape[1])
        if width == 512:
            part = t[:, :, :, col:col + 512]
        else:
            half = m.shape[1] // 2
            part = _np.concatenate([t[:, :, :, col:col + GW], t[:, :, :, half + col:half + col + GW]], 3)
        part = part.transpose(0, 2, 1, 3).reshape(2, P, CH)
        chunks.extend((part[0], part[1]))

    def rows(m):
        return list(m.reshape(-1, 2, P, D).transpose(0, 2, 1, 3).reshape(-1, P, CH))

    def feed_forward(up, down, extra=None):
        down = rows(down)
        columns(up, 0, GW)
        if extra is not None:
            columns(extra, 0)
        for j in range(1, NJ):
            columns(up, j * GW, GW)
            chunks.append(down[j - 1])
        chunks.append(down[NJ - 1])

    for kind, n in SLABS:
        columns(w["w_in"], COL0[kind] + 512 * n)
    for name in ("w_attn_out", "w_rnn_out", "w_o"):
        chunks.extend(rows(w[name]))
    feed_forward(w["w_ffn_in"], w["w_ffn_out"])
    up, down = w["ffn_w_in_2"], w["ffn_w_out_2"]
    feed_forward(up[0, 0], down[0, 0])
    for s in range(8):
        columns(w["a_w_in_2"], (512 * s + DA) % (2 * DA))
    chunks.extend(rows(w["a_w_out_2"]))
    feed_forward(up[0, 1], down[0, 1])
    feed_forward(up[1, 0], down[1, 0], w["w_kv_2"])
    q = w["b_w_q_2"].reshape(D, 2, 2, GRP, HD).transpose(0, 1, 3, 2, 4).reshape(D, D)
    for s in range(2):
        columns(q, 512 * s)
    chunks.extend(rows(w["b_w_o_2"].reshape(2, 2, GRP, HD, D).transpose(0, 2, 1, 3, 4).reshape(D, D)))
    feed_forward(up[1, 1], down[1, 1])
    return _np.stack(chunks)


def kernel(**inputs):
    import numpy as _np
    import concourse.bacc as _bacc
    from concourse import mybir as _mybir
    from concourse.bass_utils import run_bass_kernel_spmd as _run

    arrays = {k: _np.asarray(v) for k, v in inputs.items()}
    for name in _ONE_LAYER:
        arrays[name] = arrays[name][0]
    table = arrays.pop("rel_table")
    arrays["rel_rev"] = _np.pad(table[:, 1:][:, ::-1], ((0, 0), (127, 1)), mode="edge")

    arrays["stream"] = _stream(arrays)
    rows = [arrays[name].reshape(-1, P) for name in
            ("conv_w", "conv_b", "b_rg_r", "b_rg_i", "rg_lambda", "a_b_s_2")]
    rows.append(_np.zeros((P - 72, P), arrays["x"].dtype))
    ffn, mix = arrays["ffn_norm_2"], arrays["mix_norm_2"]
    rows += [g.reshape(-1, P) for g in
             (arrays["norm_mix_g"], arrays["norm_ffn_g"], ffn[0, 0], mix[0], ffn[0, 1],
              arrays["kv_norm_2"], ffn[1, 0], mix[1], ffn[1, 1], arrays["final_norm_g"])]
    rows.append(_np.zeros((P - 80, P), arrays["x"].dtype))
    arrays["params"] = _np.concatenate(rows)

    nc = _bacc.Bacc("TRN2", target_bir_lowering=False, num_devices=1)
    feed, d = {}, {}
    for name in _INS:
        a = _np.ascontiguousarray(arrays[name])
        feed[f"in_{name}"] = a
        d[name] = nc.dram_tensor(f"in_{name}", a.shape, _mybir.dt.from_np(a.dtype),
                                 kind="ExternalInput").ap()
    out = nc.dram_tensor("out_0", (S, D), F32, kind="ExternalOutput").ap()
    build(nc, d, out)
    r = _run(nc, [feed], core_ids=[0])
    return r.results[0]["out_0"].reshape(1, S, D)
```
